# Optimizing a Trainium2 kernel written in Bass

```python
import math
import jax
import jax.numpy as jnp
from jax import lax
import numpy as np

D_MODEL = 1024
BATCH = 1
SEQ = 128
DEPTH = 1
DEC_BATCH = 1
DEC_SEQ = 512
PAST_LEN = 128

GRID_W = 64
HG_HEADS = 4
HG_DK = 128
HG_DV = 128
HG_CHUNK = 64
DA_HEADS = 4
DA_DQK = 64
DA_DV = 2 * DA_DQK
Q_BLOCK = 128
N_EXPERTS = 16
EC_CAPACITY = 2
D_FF_EXPERT = 1024
ROPE_BASE = 10000.0
EPS = 1e-6
HG_W = HG_HEADS * HG_DK
HG_WV = HG_HEADS * HG_DV
DA_WQK = DA_HEADS * 2 * DA_DQK
DA_WV = DA_HEADS * DA_DV
SPLIT_SIZES = (HG_W, HG_W, HG_W, HG_WV, HG_WV, DA_WQK, DA_WQK, DA_WV, 2 * D_MODEL)
N_IN = sum(SPLIT_SIZES)

kernel_name = 'hybrid_hgrn2_diffattn_ec_moe_diffusion_step'

def rms_norm(x, w):
    xf = x.astype(jnp.float32)
    y = xf * lax.rsqrt(jnp.mean(xf * xf, axis=-1, keepdims=True) + EPS)
    return (y * w.astype(jnp.float32)).astype(x.dtype)

def axial_rope_tables(rows):
    n_freq = DA_DQK // 4
    inv = ROPE_BASE ** (-jnp.arange(n_freq, dtype=jnp.float32) / n_freq)
    row = jnp.repeat(jnp.arange(rows, dtype=jnp.float32), GRID_W)
    col = jnp.tile(jnp.arange(GRID_W, dtype=jnp.float32), rows)
    ang = jnp.stack([row[:, None] * inv, col[:, None] * inv], axis=1)
    return jnp.cos(ang), jnp.sin(ang)

def apply_axial_rope(x, cos, sin):
    B, T, H, M, _ = x.shape
    xr = x.reshape(B, T, H, M, 2, 2, DA_DQK // 4)
    x1, x2 = xr[..., 0, :], xr[..., 1, :]
    c = cos.astype(x.dtype)[None, :, None, None]
    s = sin.astype(x.dtype)[None, :, None, None]
    out = jnp.stack([x1 * c - x2 * s, x2 * c + x1 * s], axis=-2)
    return out.reshape(x.shape)

def hgrn2_scan(q, f, i, s0):
    B, T, H, dk = q.shape
    dv = i.shape[-1]
    nc = T // HG_CHUNK

    def chunks(a):
        return a.astype(jnp.float32).reshape(B, nc, HG_CHUNK, H, a.shape[-1]).transpose(1, 0, 3, 2, 4)

    ff = f.astype(jnp.float32)
    mask = jnp.tril(jnp.ones((HG_CHUNK, HG_CHUNK), dtype=bool))[None, None, :, :, None]

    def step(S, inp):
        qc, lfc, kc, vc = inp
        b = jnp.cumsum(lfc, axis=2)
        inter = jnp.einsum('bhtd,bhde->bhte', qc * jnp.exp(b), S)
        rel = jnp.where(mask, b[:, :, :, None, :] - b[:, :, None, :, :], -jnp.inf)
        attn = jnp.einsum('bhtd,bhtsd,bhsd->bhts', qc, jnp.exp(rel), kc)
        o = inter + jnp.einsum('bhts,bhse->bhte', attn, vc)
        bL = b[:, :, -1]
        S = jnp.exp(bL)[..., None] * S + jnp.einsum('bhsd,bhse->bhde', kc * jnp.exp(bL[:, :, None] - b), vc)
        return S, o

    S, o = lax.scan(step, s0.astype(jnp.float32),
                    (chunks(q), chunks(jnp.log(ff)), chunks(1.0 - ff), chunks(i)))
    o = o.transpose(1, 0, 3, 2, 4).reshape(B, T, H, dv)
    return o, S

def hgrn2_branch(hq, hff, hfb, hi, hg, lb, norm_w, s0):
    B, T, _ = hq.shape
    q = jax.nn.silu(hq).reshape(B, T, HG_HEADS, HG_DK)
    i = hi.reshape(B, T, HG_HEADS, HG_DV)

    def forget(z, lbd):
        f = lbd + (1.0 - lbd) * jax.nn.sigmoid(z.astype(jnp.float32))
        return f.reshape(B, T, HG_HEADS, HG_DK)

    o_f, s_f = hgrn2_scan(q, forget(hff, lb[0]), i, s0[:, 0])
    o_b, s_b = hgrn2_scan(q[:, ::-1], forget(hfb, lb[1])[:, ::-1], i[:, ::-1], s0[:, 1])
    o = rms_norm(o_f + o_b[:, ::-1], norm_w).astype(hq.dtype).reshape(B, T, HG_WV)
    return o * jax.nn.silu(hg), jnp.stack([s_f, s_b], axis=1)

def diff_attention(q, k, v, lam, lam_init, subln_w):
    B, Tq, H, _, d = q.shape
    nb = Tq // Q_BLOCK
    qb = q.reshape(B, nb, Q_BLOCK, H, 2, d).transpose(1, 0, 2, 3, 4, 5)
    scale = d ** -0.5

    def block(qblk):
        s = jnp.einsum('bqhmd,bkhmd->bhmqk', qblk, k, preferred_element_type=jnp.float32) * scale
        p = jax.nn.softmax(s, axis=-1)
        a = p[:, :, 0] - lam * p[:, :, 1]
        return jnp.einsum('bhqk,bkhe->bqhe', a.astype(v.dtype), v)

    o = lax.map(block, qb)
    o = o.transpose(1, 0, 2, 3, 4).reshape(B, Tq, H, DA_DV)
    o = rms_norm(o, subln_w) * (1.0 - lam_init)
    return o.reshape(B, Tq, DA_WV)

def mixer(h, w_in, b_gate, lb, hgrn_norm_w, qk_norm_w, lam, lam_init, subln_w,
          w_bh, w_ba, w_out, ctx_k, ctx_v, s0, rope):
    B, T, _ = h.shape
    split_at = [int(s) for s in np.cumsum(SPLIT_SIZES)[:-1]]
    hq, hff, hfb, hi, hg, dq, dk, dv, gl = jnp.split(h @ w_in, split_at, axis=-1)
    o_h, s_new = hgrn2_branch(hq, hff, hfb, hi, hg, lb, hgrn_norm_w, s0)
    q = rms_norm(dq.reshape(B, T, DA_HEADS, 2, DA_DQK), qk_norm_w[0])
    k = rms_norm(dk.reshape(B, T, DA_HEADS, 2, DA_DQK), qk_norm_w[1])
    v = dv.reshape(B, T, DA_HEADS, DA_DV)
    if rope is None:
        keys, vals = k, v
    else:
        q = rope(q)
        keys = jnp.concatenate([ctx_k.astype(k.dtype), rope(k)], axis=1)
        vals = jnp.concatenate([ctx_v.astype(v.dtype), v], axis=1)
    o_a = diff_attention(q, keys, vals, lam, lam_init, subln_w)
    g = jax.nn.sigmoid((gl + b_gate).astype(jnp.float32)).astype(h.dtype)
    g_h, g_a = jnp.split(g, 2, axis=-1)
    merged = g_h * (o_h @ w_bh) + g_a * (o_a @ w_ba)
    return merged @ w_out, k, v, s_new

def ec_moe(h, router_w, w_gate, w_up, w_down):
    B, T, D = h.shape
    cap = EC_CAPACITY * T // N_EXPERTS
    aff = jax.nn.softmax(jnp.einsum('btd,de->bte', h, router_w, preferred_element_type=jnp.float32), axis=-1)
    gate, idx = lax.top_k(jnp.swapaxes(aff, 1, 2), cap)
    flat = idx.reshape(B, N_EXPERTS * cap)
    xg = jnp.take_along_axis(h, flat[..., None], axis=1).reshape(B, N_EXPERTS, cap, D)
    a = jax.nn.silu(jnp.einsum('becd,edf->becf', xg, w_gate)) * jnp.einsum('becd,edf->becf', xg, w_up)
    y = jnp.einsum('becf,efd->becd', a, w_down) * gate[..., None].astype(h.dtype)
    return jnp.zeros_like(h).at[jnp.arange(B)[:, None], flat].add(y.reshape(B, N_EXPERTS * cap, D))

def trunk_layer(x, mod, norm1_w, norm2_w, mp, moe_p, ctx_k, ctx_v, s0, rope):
    sh1, sc1, g1, sh2, sc2, g2 = jnp.split(mod, 6, axis=-1)
    h = rms_norm(x, norm1_w) * (1.0 + sc1) + sh1
    y, k, v, s_new = mixer(h, *mp, ctx_k, ctx_v, s0, rope)
    x = x + g1 * y
    h = rms_norm(x, norm2_w) * (1.0 + sc2) + sh2
    x = x + g2 * ec_moe(h, *moe_p)
    return x, k, v, s_new

def setup_inputs(seed: int = 0) -> dict:
    key = jax.random.key(seed)
    ks = jax.random.split(key, 26)

    def nrm(k, shape, s):
        return jax.random.normal(k, shape, jnp.float32) * s

    D = D_MODEL
    return {
        'x_prompt': nrm(ks[0], (BATCH, SEQ, D), 1.0),
        'x_sample': nrm(ks[1], (DEC_BATCH, DEC_SEQ, D), 1.0),
        'cache_k': nrm(ks[2], (DEC_BATCH, DEPTH, PAST_LEN, DA_HEADS, 2, DA_DQK), 1.0),
        'cache_v': nrm(ks[3], (DEC_BATCH, DEPTH, PAST_LEN, DA_HEADS, DA_DV), 1.0),
        'state_hgrn': nrm(ks[4], (DEC_BATCH, DEPTH, 2, HG_HEADS, HG_DK, HG_DV), 0.5),
        'c': nrm(ks[5], (DEC_BATCH, D), 1.0),
        'c_ctx': nrm(ks[6], (D,), 1.0),
        'norm1_w': 1.0 + nrm(ks[7], (DEPTH, D), 0.02),
        'norm2_w': 1.0 + nrm(ks[8], (DEPTH, D), 0.02),
        'w_mod': nrm(ks[9], (DEPTH, D, 6 * D), 0.5 * D ** -0.5),
        'b_mod': nrm(ks[10], (DEPTH, 6 * D), 0.02),
        'w_in': nrm(ks[11], (DEPTH, D, N_IN), D ** -0.5),
        'b_gate': nrm(ks[12], (DEPTH, 2 * D), 0.02),
        'hgrn_lb_logits': nrm(ks[13], (2, DEPTH + 1, HG_W), 0.1),
        'hgrn_norm_w': 1.0 + nrm(ks[14], (DEPTH, HG_HEADS, HG_DV), 0.02),
        'qk_norm_w': 1.0 + nrm(ks[15], (DEPTH, 2, DA_DQK), 0.02),
        'diff_lambda': nrm(ks[16], (DEPTH, 4, DA_DQK), 0.1),
        'diff_subln_w': 1.0 + nrm(ks[17], (DEPTH, DA_DV), 0.02),
        'w_branch_hgrn': nrm(ks[18], (DEPTH, HG_WV, D), HG_WV ** -0.5),
        'w_branch_attn': nrm(ks[19], (DEPTH, DA_WV, D), DA_WV ** -0.5),
        'w_out': nrm(ks[20], (DEPTH, D, D), D ** -0.5),
        'router_w': nrm(ks[21], (DEPTH, D, N_EXPERTS), D ** -0.5),
        'w_exp_gate': nrm(ks[22], (DEPTH, N_EXPERTS, D, D_FF_EXPERT), D ** -0.5),
        'w_exp_up': nrm(ks[23], (DEPTH, N_EXPERTS, D, D_FF_EXPERT), D ** -0.5),
        'w_exp_down': nrm(ks[24], (DEPTH, N_EXPERTS, D_FF_EXPERT, D), D_FF_EXPERT ** -0.5),
    }

def reference(x_prompt, x_sample, cache_k, cache_v, state_hgrn, c, c_ctx,
              norm1_w, norm2_w, w_mod, b_mod, w_in, b_gate, hgrn_lb_logits, hgrn_norm_w,
              qk_norm_w, diff_lambda, diff_subln_w, w_branch_hgrn, w_branch_attn, w_out,
              router_w, w_exp_gate, w_exp_up, w_exp_down):
    lb_all = jnp.cumsum(jax.nn.softmax(hgrn_lb_logits.astype(jnp.float32), axis=1), axis=1)
    rows = x_sample.shape[1] // GRID_W
    cos, sin = axial_rope_tables(rows)

    def rope(t):
        return apply_axial_rope(t, cos, sin)

    cond_ctx = jax.nn.silu(c_ctx)[None]
    cond_lat = jax.nn.silu(c)
    s0_ctx = jnp.zeros((x_prompt.shape[0], 2, HG_HEADS, HG_DK, HG_DV), jnp.float32)
    yp, ys = x_prompt, x_sample
    k_list, v_list, s_list = [], [], []
    for l in range(DEPTH):
        lam_init = 0.8 - 0.6 * math.exp(-0.3 * l)
        lv = diff_lambda[l].astype(jnp.float32)
        lam = jnp.exp(jnp.sum(lv[0] * lv[1])) - jnp.exp(jnp.sum(lv[2] * lv[3])) + lam_init
        mp = (w_in[l], b_gate[l], lb_all[:, l], hgrn_norm_w[l], qk_norm_w[l], lam, lam_init,
              diff_subln_w[l], w_branch_hgrn[l], w_branch_attn[l], w_out[l])
        moe_p = (router_w[l], w_exp_gate[l], w_exp_up[l], w_exp_down[l])
        mod_ctx = (cond_ctx @ w_mod[l] + b_mod[l])[:, None, :]
        yp, k_l, v_l, s_l = trunk_layer(yp, mod_ctx, norm1_w[l], norm2_w[l], mp, moe_p,
                                        None, None, s0_ctx, None)
        k_list.append(k_l)
        v_list.append(v_l)
        s_list.append(s_l.astype(x_prompt.dtype))
        mod_lat = (cond_lat @ w_mod[l] + b_mod[l])[:, None, :]
        ys, _, _, _ = trunk_layer(ys, mod_lat, norm1_w[l], norm2_w[l], mp, moe_p,
                                  cache_k[:, l], cache_v[:, l], state_hgrn[:, l], rope)
    new_cache_k = jnp.stack(k_list, axis=1)
    new_cache_v = jnp.stack(v_list, axis=1)
    new_state_hgrn = jnp.stack(s_list, axis=1)
    return (yp, ys, new_cache_k, new_cache_v, new_state_hgrn)


_drawn_inputs = setup_inputs


def setup_inputs(seed=0):
    import zlib

    import numpy as np

    out = dict(_drawn_inputs(seed))
    spreads = {}
    factors = {'cache_k': 3.467,
     'cache_v': 2.863,
     'state_hgrn': 8.0,
     'norm1_w': 3.01,
     'norm2_w': 8.0,
     'b_gate': 8.0,
     'hgrn_norm_w': 8.0,
     'qk_norm_w': 2.776,
     'diff_lambda': 7.664,
     'diff_subln_w': 25.076}
    for name, (base, spread) in spreads.items():
        noise = np.random.default_rng([zlib.crc32(name.encode()), seed]).standard_normal(out[name].shape)
        drawn = base * np.exp(spread * noise) if base else spread * noise
        out[name] = jnp.asarray(drawn.astype(out[name].dtype))
    for name, factor in factors.items():
        out[name] = (out[name] * factor).astype(out[name].dtype)
    return out
```

```python
from contextlib import ExitStack

import concourse.bass as bass
from concourse import mybir

F32 = mybir.dt.float32
F32R = mybir.dt.float32r
U32 = mybir.dt.uint32
I32 = mybir.dt.int32
ALU = mybir.AluOpType
ACT = mybir.ActivationFunctionType
AX_X = mybir.AxisListType.X

P = 128
D = 1024
KD = D // P
NCTX, NLAT, NPAST = 128, 512, 128
T = NCTX + NLAT
NT = T // P
H = 4
DQK = 64
NE = 16
CAP_LAT, CAP_CTX = 2 * NLAT // NE, 2 * NCTX // NE
CAP = CAP_LAT + CAP_CTX
EPS = 1e-6
SCALE = DQK ** -0.5
LAM_INIT = 0.2
LEVELS = 7
C_HQ, C_FF, C_FB, C_HI, C_HG, C_DQ, C_DK, C_DV, C_GL = (512 * i for i in range(9))
TOK = [C_DQ, C_DK, C_DV, C_HI, C_HG]
K_ID, K_MASK, K_RESET, K_SEL, K_COS, K_SIN = 0, 128, 128 + 14 * 64, 1664, 2048, 2304
K_N = K_SIN + 256
K_COLS = 245


def fused_step(nc, A, outs):
    y_prompt, y_sample, new_k, new_v, new_state = outs
    xn_rows = nc.dram_tensor("xn_rows", (T, D), F32, kind="Internal").ap()
    y_rows = nc.dram_tensor("y_rows", (T, D), F32, kind="Internal").ap()

    w_in, w_mod = A["w_in"][0], A["w_mod"][0]
    x_tile = [A["x_prompt"][0]] + [A["x_sample"][0, i * P:(i + 1) * P, :] for i in range(4)]

    with ExitStack() as ctx:
        def sem(name):
            return ctx.enter_context(nc.semaphore(name))

        N_ARENA = 30680
        arena = ctx.enter_context(nc.sbuf_tensor("arena", [P, N_ARENA], F32))[:, :]
        top = [0]

        def take(n):
            a = arena[:, top[0]:top[0] + n]
            top[0] += n
            assert top[0] <= N_ARENA, (top[0], N_ARENA)
            return a

        NRAW = 3
        raw = [take(2048) for _ in range(NRAW)]
        o_x = top[0]
        X = take(12544)
        o_vso = top[0]
        v_hg = take(2560).rearrange("p (i n) -> p i n", i=NT)
        sg_flat = take(2560)
        sg = sg_flat.rearrange("p (h i n) -> p h i n", h=H, i=NT)
        oh = sg_flat.rearrange("p (h t) -> p h t", h=H)
        oa = take(2560).rearrange("p (h t) -> p h t", h=H)
        mg = arena[:, o_vso + 2560:o_vso + 7680].rearrange("p (c t) -> p c t", c=8)
        const = take(K_N)
        o_st = top[0] - 512
        take(512)
        cols = take(K_COLS)
        ident = const[:, K_ID:K_ID + 128]
        masks = const[:, K_MASK:K_MASK + 14 * 64].rearrange("p (d l j) -> p d l j", d=2, l=LEVELS)
        reset = const[:, K_RESET:K_RESET + T]
        cosT = const[:, K_COS:K_COS + 256].rearrange("p (i e) -> p i e", i=4)
        sinT = const[:, K_SIN:K_SIN + 256].rearrange("p (i e) -> p i e", i=4)
        sel = const[:, K_SEL:K_SEL + 384].rearrange("p (w n) -> p w n", w=3)
        at = [0]

        def col(n):
            at[0] += n
            return cols[:, at[0] - n:at[0]]

        n1c, n2c = col(8), col(8)
        condf = col(16).rearrange("p (k c) -> p k c", c=2)
        bcol = col(48)
        bgate = col(16)
        hnw = col(4)
        subln = col(1)
        lbl = col(16).rearrange("p (d l h) -> p d l h", d=2, l=2)
        qkw = col(128).rearrange("p (m e) -> p m e", m=2)
        cond = take(16).rearrange("p (k c) -> p k c", c=2)
        subln8 = take(1)
        lb = take(8).rearrange("p (d h) -> p d h", d=2)
        oml = take(8).rearrange("p (d h) -> p d h", d=2)
        lbt = take(16).rearrange("p (d l h) -> p d l h", d=2, l=2)
        lbs = take(8).rearrange("p (d h) -> p d h", d=2)
        lam = take(4)
        modc = take(96).rearrange("p (q c) -> p q c", c=2)
        A1 = take(16).rearrange("p (k c) -> p k c", c=2)
        A2 = take(16).rearrange("p (k c) -> p k c", c=2)
        ss1, rs1 = take(5), take(5)
        ss2, rs2 = take(5), take(5)
        ssq, rsq = take(80).rearrange("p (n e) -> p n e", e=8), take(80).rearrange("p (n e) -> p n e", e=8)
        negh = take(8)
        mx, nm, zz, rz = take(2), take(2), take(2), take(2)
        sso, rso = take(1), take(1)
        ss5, rs5 = take(5), take(5)
        rmx, rnm, rzz, rrz = take(1), take(1), take(1), take(1)
        mrow = take(512)
        state0 = arena[:, o_st:o_st + 1024].rearrange("p (d h e) -> p d h e", d=2, h=H)

        def part(base, n):
            return X[:, base:base + n]

        xt = [part(0, 1024), part(1024, 1024)]
        sq1 = part(2048, 1024)
        hf = part(3072, 1024).rearrange("p (k t) -> p k t", k=KD)
        qT = part(0, 2560).rearrange("p (h t) -> p h t", h=H)
        kT = part(2560, 2560).rearrange("p (h t) -> p h t", h=H)
        vd = part(5120, 2560).rearrange("p (i n) -> p i n", i=NT)
        ck, cv = part(7680, 512), part(8192, 512)
        ckT = part(8704, 512).rearrange("p (h t) -> p h t", h=H)
        pm = [part(9216, 640), part(9856, 640)]
        Ab = part(10496, 640)
        ATs = part(11136, 640)
        onb = part(11776, 128)
        lamv = part(11904, 256).rearrange("p (r e) -> p r e", r=4)
        lamp = part(12160, 128).rearrange("p (r e) -> p r e", r=2)
        sqq = part(9216, 512)
        qn = part(9728, 512)
        zr = part(10752, 512)
        QB = part(11264, 1280).rearrange("p (d t) -> p d t", d=2)
        sqo = part(12288, 128)
        sq5 = part(5760, 640)
        Fb = part(0, 1280).rearrange("p (d t) -> p d t", d=2)
        Kb = part(1280, 1280).rearrange("p (d t) -> p d t", d=2)
        qh = part(2560, 640)
        bb = part(3200, 1280).rearrange("p (d t) -> p d t", d=2)
        E = [part(4480, 1280).rearrange("p (d t) -> p d t", d=2), part(5760, 1280).rearrange("p (d t) -> p d t", d=2)]
        KS = part(7040, 1280).rearrange("p (d t) -> p d t", d=2)
        QC = part(8320, 640).rearrange("p (d t) -> p d t", d=2)
        attn = part(8960, 640)
        SC = part(9600, 768).rearrange("p (d j e) -> p d j e", d=2, j=3)
        SO = part(10368, 256).rearrange("p (d e) -> p d e", d=2)
        og = part(10624, 640)
        gate = part(0, 10240).rearrange("p (c t) -> p c t", c=16)
        mt = [part(10240, 640), part(10880, 640)]
        x1 = part(0, 5120).rearrange("p (i n) -> p i n", i=NT)
        yt = [part(5120, 512), part(5632, 512)]
        xn2 = [part(6144, 1024), part(7168, 1024)]
        sq2 = part(8192, 1024)
        h2 = part(9216, 1024).rearrange("p (k t) -> p k t", k=KD)
        aff = part(10240, 16)
        affT = part(10256, 640)
        wlat = part(10896, 512)
        router = part(11520, 128).rearrange("p (k e) -> p k e", k=8)
        G1 = arena[:, o_vso:o_vso + 2048].rearrange("p (c n) -> p c n", c=2)
        m0 = o_vso + 2560
        wctx = arena[:, m0:m0 + 128]
        vals = arena[:, m0 + 128:m0 + 208]
        idxf = arena[:, m0 + 208:m0 + 288]
        idxu = arena[:, m0 + 288:m0 + 368].bitcast(U32)
        gT = arena[:, m0 + 368:m0 + 384]
        iT = arena[:, m0 + 384:m0 + 400].bitcast(U32)
        gcur = arena[:, m0 + 400:m0 + 402]
        icur = arena[:, m0 + 402:m0 + 404].bitcast(U32)
        iscat = arena[:, m0 + 404:m0 + 405].bitcast(U32)
        A2f = arena[:, m0 + 512:m0 + 1152].rearrange("p (k t) -> p k t", k=KD)
        B2f = arena[:, m0 + 1152:m0 + 1792].rearrange("p (k t) -> p k t", k=KD)
        G2 = arena[:, m0 + 1792:m0 + 2816]
        xg = arena[:, m0 + 2816:m0 + 3840]
        aa = arena[:, m0 + 3840:m0 + 4864]
        assert 4864 <= 5120
        G2s = G2
        NRE = 6
        eraw = raw + [part(0, 2048), part(2048, 2048), part(4096, 2048)]
        ye = part(6144, 1024)
        xgt = part(7168, 640)
        xgt3 = xgt.rearrange("p (k t) -> p k t", k=KD)

        NHL = 3
        Wh = [ctx.enter_context(nc.sbuf_tensor(f"w_hi{s}", [P, 2048], F32R))[:, :] for s in range(NHL)]
        Wl = [ctx.enter_context(nc.sbuf_tensor(f"w_lo{s}", [P, 2048], F32R))[:, :] for s in range(NHL)]
        act_hi = ctx.enter_context(nc.sbuf_tensor("act_hi", [P, KD, T], F32R))[:, :, :]
        act_lo = ctx.enter_context(nc.sbuf_tensor("act_lo", [P, KD, T], F32R))[:, :, :]
        brow = arena[:, o_vso + 2048:o_vso + 2560]
        yq = [v_hg, arena[:, o_vso + 2560:o_vso + 5120].rearrange("p (i n) -> p i n", i=NT)]
        kctx = yq[1][:, 0, :]
        xh, xl = (w[:, 0, :].rearrange("p (k t) -> p k t", k=KD) for w in (act_hi, act_lo))
        ah, al = (w[:, 1, :].rearrange("p (k t) -> p k t", k=KD) for w in (act_hi, act_lo))

        PS = ctx.enter_context(nc.psum_tensor("ps", [P, 4096], F32))[:, :]

        def pair(n):
            return PS[:, 1024 * n:1024 * n + 1024]

        def bank(b):
            return PS[:, 512 * b:512 * b + 512]

        xpsum = pair(3).rearrange("p (k t) -> p k t", k=KD)[:, :, 0:CAP]

        def as2(a):
            return a.rearrange("p (b t) -> p b t", b=2)[:, :, 0:320]

        def halves(a):
            return a.rearrange("p (b t) -> p b t", b=2)

        full = [sem(f"psum_full{n}") for n in range(4)]
        free = [sem(f"psum_free{n}") for n in range(4)]
        ledger = [0] * 4
        USE = {}

        def use(key, pr, units=2, beside=0):
            assert key not in USE
            USE[key] = (pr, ledger[pr] - beside, ledger[pr] + units, units)
            ledger[pr] += units

        PIECES, RAWNO, SPLITNO, RELEASE = [], {}, {}, {}

        def piece(key, srcs, split=True):
            RAWNO[key] = len(PIECES)
            if split:
                SPLITNO[key] = len(SPLITNO)
            PIECES.append((key, srcs, split))

        def rows(w, c0, n, k0, k):
            return w[k0 * P:(k0 + k) * P, c0:c0 + n].rearrange("(k p) n -> p k n", p=P)

        def mod_pieces(j):
            for s in range(2):
                piece(("mod", j, s), [(0, 512, 4, rows(w_mod, 512 * j, 512, 4 * s, 4))], split=False)

        ITER = [(h, i) for h in range(H) for i in range(NT)]
        NI = len(ITER)
        STEPS = []
        for j in range(4):
            mod_pieces(j)
            STEPS.append(("mod", j))
        for i in range(NT):
            STEPS.append(("xT", i))
        STEPS.append(("split",))
        for g in range(5):
            for s in range(2):
                piece(("tok", g, s), [(0, 512, 4, rows(w_in, TOK[g], 512, 4 * s, 4))])
                STEPS.append(("tok", g, s))
                if s == 0 and g in (1, 2):
                    STEPS.append(("qkT", g - 1))
        STEPS.append(("da", -1))
        for n in range(NI + 1):
            STEPS.append(("da", n))

        def fproj(h):
            STEPS.append(("f", h, 0))
            STEPS.append(("f", h, 1))

        def qproj(h):
            STEPS.append(("q", h))

        def head_pieces(h):
            piece(("f", h), [(0, 128, 8, rows(w_in, C_FF + 128 * h, 128, 0, 8)), (1024, 128, 8, rows(w_in, C_FB + 128 * h, 128, 0, 8))])
            piece(("q", h), [(0, 128, 8, rows(w_in, C_HQ + 128 * h, 128, 0, 8))])

        def gl_piece(c):
            piece(("gl", c), [(0, 256, 8, rows(w_in, C_GL + 256 * c, 256, 0, 8))])

        head_pieces(0)
        head_pieces(1)
        mod_pieces(6)
        head_pieces(2)
        mod_pieces(7)
        head_pieces(3)
        mod_pieces(8)
        gl_piece(0)
        gl_piece(1)
        mod_pieces(9)
        gl_piece(2)
        gl_piece(3)
        mod_pieces(4)
        gl_piece(4)
        gl_piece(5)
        mod_pieces(5)
        gl_piece(6)
        gl_piece(7)
        fproj(0)
        qproj(0)
        for h in range(H):
            STEPS.append(("diag", h))
            for lv in range(LEVELS):
                STEPS.append(("lev", h, lv))
            STEPS.append(("mod", 6 + h))
            if h + 1 < H:
                fproj(h + 1)
            STEPS.append(("tail", h))
            if h + 1 < H:
                qproj(h + 1)
        LATE = [4, 5, 10, 11]
        for c in range(8):
            STEPS.append(("gl", 2 * c))
            STEPS.append(("gl", 2 * c + 1))
            if c in (1, 3):
                STEPS.append(("mod", LATE[c // 2]))
        for c in range(8):
            if c % 4 == 0:
                for b, w in enumerate((A["w_branch_hgrn"][0], A["w_branch_attn"][0])):
                    piece(("br", b, c // 4), [(0, 512, 4, rows(w, 512 * (c // 4), 512, 0, 4))])
            STEPS.append(("mrg", c))
        for n in range(2):
            for s in range(2):
                piece(("out", n, s), [(0, 512, 4, rows(A["w_out"][0], 512 * n, 512, 4 * s, 4))])
                STEPS.append(("out", n, s))
        for j in LATE[2:]:
            mod_pieces(j)
            STEPS.append(("mod", j))
        for i in range(NT):
            STEPS.append(("h2T", i))
        STEPS.append(("top",))

        for st in STEPS:
            k = st[0]
            if k == "mod":
                j = st[1]
                use(("modrow", j), 2)
                if j in LATE:
                    if j < 6:
                        use(("g1", j, 0), 2)
                        use(("g1", j, 1), 2)
                    else:
                        use(("g2", j), 2)
                else:
                    use(("modcol", j), 2)
            elif k == "xT":
                use(("xT", st[1]), 3)
            elif k in ("tok", "out") and st[2] == 0:
                for i in range(NT):
                    use((k, st[1], i), i // 2, 1, i % 2)
            elif k == "qkT":
                for i in range(NT):
                    use(("qkT", st[1], i), 3)
            elif k == "da":
                n = st[1]
                if n + 1 < NI:
                    use(("s", n + 1, 0), 0)
                    use(("s", n + 1, 1), 1)
                if 0 <= n < NI:
                    use(("AT", n), 2)
                if n >= 1:
                    use(("oaT", n - 1), 3)
                if 0 <= n < NI:
                    use(("pv", n), 3)
            elif k == "f":
                use(st, st[2])
            elif k == "q":
                use(st, 0)
            elif k == "diag":
                use(st, 3)
            elif k == "lev":
                use((*st, 0), 2, 1)
                use((*st, 1), 2, 1, 1)
            elif k == "tail":
                h = st[1]
                use(("kT", h, 0), 3)
                use(("kT", h, 1), 3)
                use(("U", h, 0), 2, 1)
                use(("U", h, 1), 2, 1, 1)
                use(("o", h), 3)
                use(("oT", h), 3)
            elif k == "gl":
                use(st, st[1] % 2)
            elif k == "mrg":
                c = st[1]
                use(("mx", c), 2 * (c % 2))
                use(("my", c), 2 * (c % 2) + 1)
            elif k == "h2T":
                use(("h2T", st[1]), 3)
                use(("rt", st[1]), 2)
                use(("affT", st[1]), 2)
            elif k == "top":
                use(("gi",), 3)

        def filled(eng, key):
            eng.wait_ge(full[USE[key][0]], USE[key][2])

        def release(ins, key):
            return ins.then_inc(free[USE[key][0]], USE[key][3])

        def begin(pe, key):
            if USE[key][1]:
                pe.wait_ge(free[USE[key][0]], USE[key][1])

        def wrote(ins, key):
            return ins.then_inc(full[USE[key][0]], USE[key][3])

        NSM = 5
        s_small = sem("s_small")
        s_raw = [sem(f"s_raw{s}") for s in range(NRAW)]
        s_hi, s_lo = sem("s_hi"), sem("s_lo")
        s_wused = sem("s_wused")
        s_rused = sem("s_rused")
        s_x = [sem("s_xin0"), sem("s_xin1")]
        s_sq1, s_r1, s_xn, s_hf, s_hh, s_hl = (sem(n) for n in ("s_sq1", "s_r1", "s_xn", "s_hf", "s_hh", "s_hl"))
        s_cond, s_mrow, s_lbe, s_lame = sem("s_cond"), sem("s_mrow"), sem("s_lbe"), sem("s_lame")
        s_neg = sem("s_neg")
        s_pool = sem("s_pool")
        s_v = sem("s_v")
        s_sqq, s_rdq, s_rq, s_qr = sem("s_sqq"), sem("s_rdq"), sem("s_rq"), sem("s_qr")
        s_nm, s_p, s_A, s_AT = sem("s_nm"), sem("s_p"), sem("s_A"), sem("s_AT")
        s_sqo, s_ro, s_on = sem("s_sqo"), sem("s_ro"), sem("s_on")
        s_sig, s_f, s_ln, s_sub, s_e, s_qk, s_attn = (sem(n) for n in ("s_sig", "s_f", "s_ln", "s_sub", "s_e", "s_qk", "s_attn"))
        s_qsilu, s_ksum = sem("s_qsilu"), sem("s_ksum")
        s_eb, s_ebl, s_ksb, s_qb, s_S, s_so = (sem(n) for n in ("s_eb", "s_ebl", "s_ksb", "s_qb", "s_S", "s_so"))
        s_sq5, s_rd5, s_r5, s_og, s_tl = sem("s_sq5"), sem("s_rd5"), sem("s_r5"), sem("s_og"), sem("s_tl")
        s_oth, s_otl, s_mgh, s_mgl, s_mg = (sem(n) for n in ("s_oth", "s_otl", "s_mgh", "s_mgl", "s_mg"))
        s_x1in, s_x1, s_sq2, s_r2, s_xn2, s_h2, s_rm, s_re, s_aff = (
            sem(n) for n in ("s_x1in", "s_x1", "s_sq2", "s_r2", "s_xn2", "s_h2", "s_rm", "s_re", "s_aff"))
        s_xrow = [sem("s_xrow0"), sem("s_xrow1")]
        s_gi, s_gt, s_kc = sem("s_gi"), sem("s_gt"), sem("s_kc")
        s_nk, s_nv, s_st, s_yrow, s_yout = (sem(n) for n in ("s_nk", "s_nv", "s_st", "s_yrow", "s_yout"))
        s_st0, s_go = sem("s_st0"), sem("s_go")
        s_brow, s_lbt, s_scan = sem("s_brow"), sem("s_lbt"), sem("s_scan")
        s_icq, s_xgm, s_gm, s_um, s_ebl2, s_tbl = (sem(n) for n in ("s_icq", "s_xgm", "s_gm", "s_um", "s_ebl2", "s_tbl"))
        s_er = [sem(f"s_er{s}") for s in range(NRE)]
        s_eh, s_el, s_eu = sem("s_eh"), sem("s_el"), sem("s_eu")
        s_icp, s_gath, s_xgT, s_xgf, s_xgh, s_xgl = (sem(n) for n in ("s_icp", "s_gath", "s_xgT", "s_xgf", "s_xgh", "s_xgl"))
        s_gt_e, s_up, s_dn, s_silu, s_a, s_aT, s_afc, s_ahi, s_alo, s_y, s_scat, s_gcp = (sem(n) for n in (
            "s_gt_e", "s_up", "s_dn", "s_silu", "s_a", "s_aT", "s_afc", "s_ahi", "s_alo", "s_y", "s_scat", "s_gcp"))

        rawfill = {}
        count = [0] * NRAW
        for n, (key, srcs, split) in enumerate(PIECES):
            count[n % NRAW] += 16 * len(srcs)
            rawfill[key] = count[n % NRAW]
        modno = {}
        for key, srcs, split in PIECES:
            if not split:
                modno[key] = len(modno) + 1

        used, nw, nr = {}, 0, 0
        for key, _, _ in PIECES:
            k = key[0]
            if k == "mod":
                if key[2] == 0:
                    nr += 1
                    used[key] = (s_rused, nr)
                else:
                    used[key] = (full[2], USE[("modrow", key[1])][2])
            elif k in ("tok", "out"):
                if key[2] == 0:
                    nw += 1
                    used[key] = (s_wused, nw)
                else:
                    used[key] = (full[2], USE[(k, key[1], 4)][2])
            elif k == "f":
                used[key] = (full[1], USE[("f", key[1], 1)][2])
            elif k == "q":
                used[key] = (full[0], USE[key][2])
            elif k == "gl":
                used[key] = (full[1], USE[("gl", 2 * key[1] + 1)][2])
            elif k == "br":
                c = 4 * key[2] + 3
                used[key] = (full[USE[("my", c)][0]], USE[("my", c)][2])

        def landed(eng, key):
            eng.wait_ge(s_raw[RAWNO[key] % NRAW], rawfill[key])

        def rawv(key):
            return raw[RAWNO[key] % NRAW]

        def hl(key):
            s = SPLITNO[key] % NHL
            return Wh[s], Wl[s]

        SPLITS = [k for k, _, sp in PIECES if sp]
        AHEAD = 2
        before = {}
        nxt = 0
        for n, st in enumerate(STEPS):
            k = st[0]
            last = None
            if k in ("tok", "out"):
                last = SPLITNO[st]
            elif k == "f" and st[2] == 0:
                last = SPLITNO[("f", st[1])]
            elif k == "q":
                last = SPLITNO[st]
            elif k == "gl" and st[1] % 2 == 0:
                last = SPLITNO[("gl", st[1] // 2)]
            elif k == "mrg" and st[1] % 4 == 0:
                last = SPLITNO[("br", 1, st[1] // 4)]
            todo = []
            if last is not None:
                while nxt < len(SPLITS) and nxt <= last + (AHEAD if k != "mrg" else 1):
                    todo.append(SPLITS[nxt])
                    nxt += 1
            before[n] = todo
        assert nxt == len(SPLITS)

        def width(key):
            return 1024 if key[0] == "q" else 2048

        block = ctx.enter_context(nc.Block())

        @block.sync
        def _(sp):
            small = [
                (const, A["const"]),
                (cols, A["cols"]),
                (lamv, A["diff_lambda"][0].partition_broadcast(P)),
                (ckT.rearrange("p h t -> p (h t)"), A["ckT"]),
                (cv, A["cache_v"][0, 0].rearrange("t h d -> t (h d)")),
            ]
            assert len(small) == NSM
            for dst, src in small[0:2]:
                sp.dma_start(dst, src).then_inc(s_small, 16)

            def load(n):
                key, srcs, split = PIECES[n]
                if n >= NRAW:
                    old = PIECES[n - NRAW][0]
                    if old in SPLITNO:
                        sp.wait_ge(s_lo, SPLITNO[old] + 1)
                    else:
                        sp.wait_ge(*used[old])
                for off, cols, k, src in srcs:
                    dst = raw[n % NRAW][:, off:off + cols * k].rearrange("p (k n) -> p k n", k=k)
                    sp.dma_start(dst, src).then_inc(s_raw[n % NRAW], 16)

            def load_x(i):
                if i >= 2:
                    filled(sp, ("xT", i - 2))
                sp.dma_start(xt[i % 2], x_tile[i]).then_inc(s_x[i % 2], 16)

            def load_brow(j):
                sp.dma_start(brow[0:1, :], A["b_mod"][0:1, 512 * j:512 * j + 512]).then_inc(s_brow, 16)

            load(0)
            load(1)
            load_x(0)
            load(2)
            load_x(1)
            for dst, src in small[2:]:
                sp.dma_start(dst, src).then_inc(s_small, 16)
            for n in range(3, 8):
                load(n)
            for i in range(2, NT):
                load_x(i)
            out_at = {"nk": RAWNO[("tok", 3, 1)], "nv": RAWNO[("tok", 4, 1)]}
            st_at = {RAWNO[("q", 2)]: 0, RAWNO[("q", 3)]: 1, RAWNO[("gl", 1)]: 2, RAWNO[("gl", 2)]: 3}
            for n in range(8, len(PIECES)):
                if n == out_at["nk"]:
                    sp.wait_ge(s_qr, 2 * NT)
                    sp.dma_start(new_k[0, 0].rearrange("t h m d -> t (h m d)"), kctx).then_inc(s_nk, 16)
                    for d in range(2):
                        sp.dma_start(state0[:, d], A["state_hgrn"][0, 0, d].rearrange("h k e -> k h e")).then_inc(s_st0, 16)
                if n == out_at["nv"]:
                    sp.wait_ge(free[USE[("tok", 2, 0)][0]], USE[("tok", 2, 0)][2])
                    sp.dma_start(new_v[0, 0].rearrange("t h d -> t (h d)"), vd[:, 0, :]).then_inc(s_nv, 16)
                if n in (RAWNO[("gl", 2)], RAWNO[("gl", 4)]):
                    filled(sp, ("o", H - 1) if n == RAWNO[("gl", 2)] else ("g1", 4, 1))
                    load_brow(4 if n == RAWNO[("gl", 2)] else 5)
                if n in st_at:
                    h = st_at[n]
                    sp.wait_ge(s_so, 2 * (h + 1))
                    sp.dma_start(new_state[0, 0, :, h].rearrange("d k e -> k d e"), SO).then_inc(s_st, 16)
                load(n)
                if n == RAWNO[("out", 0, 0)]:
                    sp.wait_ge(s_mg, 8)
                    for i in range(NT):
                        sp.dma_start(x1[:, i, :], x_tile[i]).then_inc(s_x1in, 16)
                    sp.dma_start(router, A["router_w"][0].rearrange("(k p) e -> p k e", p=P)).then_inc(s_x1in, 16)
            filled(sp, ("g1", 5, 1))
            load_brow(10)
            filled(sp, ("g2", 10))
            load_brow(11)
            for i in range(NT):
                sp.wait_ge(s_x1, NT + i + 1)
                sp.dma_start(y_rows[i * P:(i + 1) * P, :], x1[:, i, :]).then_inc(s_yrow, 16)
            for i in range(NT):
                sp.wait_ge(s_xn2, i + 1)
                sp.dma_start(xn_rows[i * P:(i + 1) * P, :], xn2[i % 2]).then_inc(s_xrow[i % 2], 16)

            wg, wu, wd = (A[n][0] for n in ("w_exp_gate", "w_exp_up", "w_exp_down"))

            def epiece(w, e, k, slot):
                src = w[bass.ds(e, 1), bass.ts(k, 2 * P), :].rearrange("a (k p) n -> p (a k) n", p=P)
                sp.dma_start(eraw[slot].rearrange("p (k n) -> p k n", k=2), src).then_inc(s_er[slot], 16)

            sp.wait_ge(s_lo, len(SPLITS))
            sp.wait_ge(*used[("mod", LATE[-1], 1)])
            sp.wait_ge(s_gt, 2)
            sp.wait_ge(s_yrow, 16 * NT)
            for s in range(2):
                sp.wait_ge(s_xrow[s], 16 * (3 - s))
            for n in range(8):
                if n >= NRE:
                    sp.wait_ge(s_el, n - NRE + 1)
                epiece(wg if n < 4 else wu, 0, n % 4, n % NRE)
            with sp.Fori(1, NE) as e:
                for j in range(12):
                    sp.wait_ge(s_el, e * 12 + (j - 4 - NRE + 1))
                    if j < 4:
                        epiece(wg, e, j, (j + 2) % NRE)
                    elif j < 8:
                        epiece(wu, e, j - 4, (j + 2) % NRE)
                    else:
                        epiece(wd, e - 1, j - 8, (j + 2) % NRE)
            for j in range(4):
                sp.wait_ge(s_el, 188 + j - NRE + 1)
                epiece(wd, NE - 1, j, (188 + j) % NRE)
            sp.wait_ge(s_scat, 16 * NE)
            sp.dma_start(y_prompt[0], y_rows[0:NCTX, :]).then_inc(s_yout, 16)
            sp.dma_start(y_sample[0], y_rows[NCTX:T, :]).then_inc(s_yout, 16)
            sp.wait_ge(s_nk, 16)
            sp.wait_ge(s_nv, 16)
            sp.wait_ge(s_st, 16 * H)
            sp.wait_ge(s_yout, 32)

        @block.gpsimd
        def _(pool):
            g = nc.gpsimd
            chain = [0]

            def link(ins):
                chain[0] += 1
                ins.then_inc(s_pool, 1)
                pool.wait_ge(s_pool, chain[0])

            g.memset(negh, -0.5).then_inc(s_neg, 1)
            pool.wait_ge(s_neg, 1)

            def rroot(out, ss, n, sig, w):
                link(g.tensor_scalar(out, ss, 1.0 / n, EPS, ALU.mult, ALU.add))
                g.tensor_tensor(out, out, negh[:, 0:w], ALU.pow).then_inc(sig, 1)

            for i in range(NT):
                pool.wait_ge(s_sq1, i + 1)
                rroot(rs1[:, i:i + 1], ss1[:, i:i + 1], D, s_r1, 1)
            for n in range(2 * NT):
                pool.wait_ge(s_rdq, n + 1)
                rroot(rsq[:, n, :], ssq[:, n, :], DQK, s_rq, 8)
            for n in range(NI):
                pool.wait_ge(s_sqo, n + 1)
                if n:
                    pool.wait_ge(free[3], USE[("pv", n - 1)][2])
                rroot(rso, sso, P, s_ro, 1)
            for h in range(H):
                pool.wait_ge(s_rd5, h + 1)
                rroot(rs5, ss5, P, s_r5, 5)
            for i in range(NT):
                pool.wait_ge(s_sq2, i + 1)
                rroot(rs2[:, i:i + 1], ss2[:, i:i + 1], D, s_r2, 1)

            pool.wait_ge(s_gt, 2)
            for s in range(2):
                pool.wait_ge(s_xrow[s], 16 * (3 - s))
            pool.wait_ge(s_yrow, 16 * NT)

            def fetch():
                g.indirect_dma_start(out=xg[0:CAP, :], out_offset=None, in_=xn_rows,
                                     in_offset=bass.IndirectOffsetOnAxis(ap=icur[0:CAP, 0:1], axis=0)).then_inc(s_gath, 16)

            def gather(e):
                pool.wait_ge(s_xgT, e)
                g.tensor_copy(icur[0:CAP, 0:1], iT[0:CAP, bass.ds(e, 1)]).then_inc(s_icp, 1)
                pool.wait_ge(s_icp, e + 1)
                pool.sem_inc(s_go, 1)
                fetch()

            def scatter(e):
                g.tensor_copy(iscat[0:CAP, 0:1], iT[0:CAP, bass.ds(e, 1)]).then_inc(s_icq, 1)
                pool.wait_ge(s_icq, e + 1)
                pool.wait_ge(s_y, e + 1)
                pool.sem_inc(s_go, 1)
                g.indirect_dma_start(out=y_rows, out_offset=bass.IndirectOffsetOnAxis(ap=iscat[0:CAP, 0:1], axis=0),
                                     in_=ye[0:CAP, :], in_offset=None, compute_op=ALU.add).then_inc(s_scat, 16)
                pool.wait_ge(s_scat, 16 * e + 16)

            g.tensor_copy(icur[0:CAP, 0:1], iT[0:CAP, 0:1]).then_inc(s_icp, 1)
            pool.wait_ge(s_icp, 1)
            fetch()
            gather(1)
            gather(2)
            with pool.Fori(2, NE - 1) as e:
                gather(e + 1)
                scatter(e - 2)
            for e in range(NE - 3, NE):
                scatter(e)

        @block.scalar
        def _(act):
            a = nc.scalar
            act.wait_ge(s_small, 16 * NSM)
            a.activation(cond, condf, ACT.Silu).then_inc(s_cond, 1)

            def square_x(t):
                act.wait_ge(s_x[t % 2], 16 * (t // 2 + 1))
                if t:
                    act.wait_ge(s_sq1, t)
                a.activation(sq1, xt[t % 2], ACT.Square, accum_out=ss1[:, t:t + 1]).then_inc(s_sq1, 1)

            square_x(0)
            square_x(1)
            nsplit = [0]

            def hi(key):
                n, w = SPLITNO[key], width(key)
                landed(act, key)
                if n >= NHL:
                    act.wait_ge(*used[SPLITS[n - NHL]])
                a.activation(hl(key)[0][:, 0:w], rawv(key)[:, 0:w], ACT.Copy).then_inc(s_hi, 1)

            def evac(dst, key, func=ACT.Copy, src=None, **kw):
                filled(act, key)
                release(a.activation(dst, src, func, **kw), key)

            def da_exp(n):
                h, i = ITER[n]
                nk = 640 if i else 128
                act.wait_ge(s_nm, n + 1)
                if n:
                    act.wait_ge(s_A, n)
                for m in range(2):
                    filled(act, ("s", n, m))
                    release(a.activation(pm[m][:, 0:nk], pair(m)[:, 0:nk], ACT.Exp, scale=SCALE, bias=nm[:, m:m + 1],
                                         accum_out=zz[:, m:m + 1]), ("s", n, m))

            for n, st in enumerate(STEPS):
                for key in before[n]:
                    hi(key)
                k = st[0]
                if k == "mod":
                    j = st[1]
                    evac(mrow[0:2, :], ("modrow", j), src=bank(4)[0:2, :])
                    if j in (4, 5):
                        for c in range(2):
                            evac(G1[:, c, 512 * (j - 4):512 * (j - 3)], ("g1", j, c), src=bank(4))
                    if j in (10, 11):
                        act.wait_ge(s_mgl, 2)
                        evac(G2s[0:CAP, 512 * (j - 10):512 * (j - 9)], ("g2", j), src=bank(4)[0:CAP, :])
                elif k == "xT":
                    i = st[1]
                    act.wait_ge(s_hf, i + 1)
                    a.activation(act_hi[:, :, P * i:P * i + P], hf, ACT.Copy).then_inc(s_hh, 1)
                    if i + 2 < NT:
                        square_x(i + 2)
                elif k == "tok" and st[2] == 1:
                    g = st[1]
                    for i in range(NT):
                        key = ("tok", g, i)
                        if g < 2:
                            filled(act, key)
                            if g or i:
                                act.wait_ge(s_rdq, 5 * g + i)
                            a.activation(sqq, bank(i), ACT.Square).then_inc(s_sqq, 1)
                        elif g == 2:
                            evac(vd[:, i, :], key, src=bank(i))
                        elif g == 3:
                            evac(v_hg[:, i, :], key, src=bank(i))
                        else:
                            if i == 0:
                                act.wait_ge(s_nk, 16)
                            evac(sg[:, :, i, :], key, ACT.Silu, src=bank(i).rearrange("p (h n) -> p h n", h=H))
                elif k == "qkT":
                    act.wait_ge(s_hl, NT)
                    for i in range(NT):
                        dst = (qT, kT)[st[1]][:, :, P * i:P * i + P]
                        evac(dst, ("qkT", st[1], i), src=pair(3)[:, 0:512].rearrange("p (h t) -> p h t", h=H))
                elif k == "da":
                    n = st[1]
                    if n == -1:
                        act.wait_ge(s_lame, 1)
                        a.activation(lam[:, 2:4], lam[:, 0:2], ACT.Exp).then_inc(s_lame, 1)
                        act.wait_ge(s_lbt, 1)
                        a.activation(lbt, lbt, ACT.Exp).then_inc(s_lbe, 1)
                    if n + 1 < NI:
                        da_exp(n + 1)
                    if 0 <= n < NI:
                        nk = 640 if ITER[n][1] else 128
                        if n:
                            filled(act, ("pv", n - 1))
                        filled(act, ("AT", n))
                        a.activation(ATs[:, 0:nk], pair(2)[:, 0:nk], ACT.Copy).then_inc(free[2], 2)
                    if n >= 1:
                        h, i = ITER[n - 1]
                        evac(oa[:, h, P * i:P * i + P], ("oaT", n - 1), src=bank(7)[:, 0:P], scale=subln8)
                    if 0 <= n < NI:
                        filled(act, ("pv", n))
                        if n:
                            act.wait_ge(s_ro, n)
                        a.activation(sqo, bank(6)[:, 0:P], ACT.Square, accum_out=sso).then_inc(s_sqo, 1)
                elif k == "f":
                    h, d = st[1], st[2]
                    if h and d == 0:
                        act.wait_ge(s_scan, h)
                    evac(halves(Fb[:, d, :]), st, ACT.Sigmoid, src=as2(pair(d)))
                elif k == "q":
                    h = st[1]
                    evac(halves(qh), st, ACT.Silu, src=as2(pair(0)))
                    act.wait_ge(s_f, h + 1)
                    a.activation(Fb, Fb, ACT.Ln).then_inc(s_ln, 1)
                elif k == "lev":
                    h, lv = st[1], st[2]
                    act.wait_ge(s_sub, LEVELS * h + lv + 1)
                    a.activation(E[lv % 2], E[lv % 2], ACT.Exp).then_inc(s_e, 1)
                elif k == "tail":
                    h = st[1]
                    act.wait_ge(s_qk, LEVELS * (h + 1))
                    a.activation(E[1], bb, ACT.Exp).then_inc(s_eb, 1)
                    act.wait_ge(s_ebl, h + 1)
                    a.activation(E[0], E[0], ACT.Exp).then_inc(s_ebl2, 1)
                    act.wait_ge(s_ksb, h + 1)
                    for d in range(2):
                        evac(E[0][:, d, :], ("kT", h, d), src=pair(3)[:, 0:T])
                    filled(act, ("o", h))
                    act.wait_ge(s_qb, h + 1)
                    a.activation(sq5, pair(3)[:, 0:T], ACT.Square).then_inc(s_sq5, 1)
                    evac(oh[:, h, :], ("oT", h), src=pair(3)[:, 0:T], scale=hnw[:, h:h + 1])
                elif k == "gl":
                    c = st[1]
                    if c == 0:
                        act.wait_ge(s_so, 2 * H)
                    evac(halves(gate[:, c, :]), st, ACT.Sigmoid, src=as2(pair(c % 2)), bias=bgate[:, c:c + 1])
                elif k == "mrg":
                    if st[1] == 0:
                        filled(act, ("gl", 15))
                        filled(act, ("gl", 14))
                        a.activation(act_hi[:, 0:4, :], oh, ACT.Copy).then_inc(s_oth, 1)
                        a.activation(act_hi[:, 4:8, :], oa, ACT.Copy).then_inc(s_oth, 1)
                    if st[1] == 7:
                        filled(act, ("my", 7))
                        filled(act, ("my", 6))
                        act.wait_ge(s_mg, 8)
                        for b in range(2):
                            a.activation(act_hi[:, 4 * b:4 * b + 4, :], mg[:, 4 * b:4 * b + 4, :], ACT.Copy).then_inc(s_mgh, 1)
                elif k == "h2T":
                    i = st[1]
                    if i == 0:
                        for t in range(NT):
                            act.wait_ge(s_x1, NT + t + 1)
                            if t:
                                act.wait_ge(s_sq2, t)
                            a.activation(sq2, x1[:, t, :], ACT.Square, accum_out=ss2[:, t:t + 1]).then_inc(s_sq2, 1)
                    act.wait_ge(s_rm, i + 1)
                    filled(act, ("rt", i))
                    release(a.activation(aff, bank(4)[:, 0:NE], ACT.Exp, bias=rnm, accum_out=rzz), ("rt", i))
                    evac(affT[0:NE, P * i:P * i + P], ("affT", i), src=bank(4)[0:NE, 0:P])

            def xhi(e):
                act.wait_ge(s_xgf, e + 1)
                a.activation(xh, xgt3, ACT.Copy).then_inc(s_xgh, 1)

            def ahi(e):
                act.wait_ge(s_aT, e + 1)
                a.activation(ah, xpsum, ACT.Copy).then_inc(s_ahi, 1)

            def silu(e):
                act.wait_ge(s_eu, e * 12)
                act.wait_ge(s_aT, e)
                a.activation(aa[0:CAP, :], pair(0)[0:CAP, :], ACT.Silu).then_inc(s_silu, 1)

            def body(e, last=False):
                for j in range(12):
                    ehi_at(e, j)
                    if j == 0:
                        ahi(e - 1)
                    if j == 6:
                        silu(e)
                    if j == 8 and not last:
                        xhi(e + 1)

            def ehi_at(e, j):
                act.wait_ge(s_er[(j + 2) % NRE], (e * 2 + (j - 4) // 6 + 1) * 16)
                act.wait_ge(s_eu, e * 12 + (j - 6))
                a.activation(Wh[(j + 2) % NHL], eraw[(j + 2) % NRE], ACT.Copy).then_inc(s_eh, 1)

            xhi(0)
            for n in range(8):
                act.wait_ge(s_er[n % NRE], 16 * (n // NRE + 1))
                if n >= NHL:
                    act.wait_ge(s_eu, n - 2)
                a.activation(Wh[n % NHL], eraw[n % NRE], ACT.Copy).then_inc(s_eh, 1)
            act.wait_ge(s_eu, 4)
            a.activation(aa[0:CAP, :], pair(0)[0:CAP, :], ACT.Silu).then_inc(s_silu, 1)
            xhi(1)
            body(1)
            with act.Fori(2, NE - 1) as e:
                body(e)
            body(NE - 1, last=True)
            for n in range(188, 192):
                act.wait_ge(s_er[n % NRE], 16 * (n // NRE + 1))
                act.wait_ge(s_eu, n - 2)
                a.activation(Wh[n % NHL], eraw[n % NRE], ACT.Copy).then_inc(s_eh, 1)
                if n == 188:
                    ahi(NE - 1)

        @block.vector
        def _(dve):
            v = nc.vector
            chain = [0]

            def link(ins):
                chain[0] += 1
                ins.then_inc(s_v, 1)
                dve.wait_ge(s_v, chain[0])

            count = {}

            def own(sig):
                count[sig.name] = count.get(sig.name, 0) + 1
                dve.wait_ge(sig, count[sig.name])

            def read(key):
                dve.wait_ge(free[USE[key][0]], USE[key][2])

            def lo(key):
                n, w = SPLITNO[key], width(key)
                dve.wait_ge(s_hi, n + 1)
                h_, l_ = hl(key)
                v.tensor_tensor(l_[:, 0:w], rawv(key)[:, 0:w], h_[:, 0:w].bitcast(F32), ALU.subtract).then_inc(s_lo, 1)

            def norm_x(t):
                dve.wait_ge(s_r1, t + 1)
                v.tensor_scalar(xt[t % 2], xt[t % 2], rs1[:, t:t + 1], None, ALU.mult).then_inc(s_xn, 1)
                own(s_xn)

            def norm_x2(t):
                dve.wait_ge(s_r2, t + 1)
                if t >= 2:
                    dve.wait_ge(s_xrow[t % 2], 16 * (t // 2))
                v.tensor_scalar(xn2[t % 2], x1[:, t, :], rs2[:, t:t + 1], None, ALU.mult).then_inc(s_xn2, 1)
                own(s_xn2)

            def sum_q(g, i):
                dve.wait_ge(s_sqq, 5 * g + i + 1)
                v.tensor_reduce(ssq[:, 5 * g + i, :], sqq.rearrange("p (g e) -> p g e", g=8), AX_X, ALU.add).then_inc(s_rdq, 1)
                own(s_rdq)

            def norm_q(g, i):
                n = 5 * g + i
                dve.wait_ge(s_rq, n + 1)
                q3 = qn.rearrange("p (g e) -> p g e", g=8)
                y = yq[g][:, i, :]
                y3 = y.rearrange("p (g e) -> p g e", g=8)
                w = qkw[:, g:g + 1, :].broadcast_to([P, 8, DQK])
                r = rsq[:, n, :].unsqueeze(2).broadcast_to([P, 8, DQK])
                release(v.tensor_tensor(q3, bank(i).rearrange("p (g e) -> p g e", g=8), r, ALU.mult), ("tok", g, i))
                read(("tok", g, i))
                dve.wait_ge(free[i // 2], USE[("tok", g, i)][2])
                if i == 0:
                    v.tensor_tensor(y3, q3, w, ALU.mult).then_inc(s_qr, 1)
                    own(s_qr)
                    return
                link(v.tensor_tensor(q3, q3, w, ALU.mult))
                cc = cosT[:, i - 1:i, :].broadcast_to([P, 8, DQK])
                link(v.tensor_tensor(y3, q3, cc, ALU.mult))
                q5 = qn.rearrange("p (g a b e) -> p g a b e", g=8, a=2, b=2)
                z5 = zr.rearrange("p (g a b e) -> p g a b e", g=8, a=2, b=2)
                s5 = sinT[:, i - 1, :].rearrange("p (g a b e) -> p g a b e", g=1, a=2, b=2)
                link(v.tensor_tensor(z5[:, :, :, 0, :], q5[:, :, :, 1, :], s5[:, :, :, 0, :].broadcast_to([P, 8, 2, 16]), ALU.mult))
                link(v.tensor_tensor(z5[:, :, :, 1, :], q5[:, :, :, 0, :], s5[:, :, :, 1, :].broadcast_to([P, 8, 2, 16]), ALU.mult))
                v.tensor_tensor(y, y, zr, ALU.add).then_inc(s_qr, 1)
                own(s_qr)

            def da_max(n):
                nk = 640 if ITER[n][1] else 128
                for m in range(2):
                    filled(dve, ("s", n, m))
                    link(v.tensor_reduce(mx[:, m:m + 1], pair(m)[:, 0:nk], AX_X, ALU.max))
                v.tensor_scalar(nm, mx, -SCALE, None, ALU.mult).then_inc(s_nm, 1)
                own(s_nm)

            def da_comb(n):
                nk = 640 if ITER[n][1] else 128
                dve.wait_ge(free[1], USE[("s", n, 1)][2])
                dve.wait_ge(free[0], USE[("s", n, 0)][2])
                link(v.reciprocal(rz, zz))
                link(v.tensor_tensor(rz[:, 1:2], rz[:, 1:2], lam[:, 0:1], ALU.mult))
                link(v.tensor_scalar(pm[1][:, 0:nk], pm[1][:, 0:nk], rz[:, 1:2], None, ALU.mult))
                if n:
                    filled(dve, ("AT", n - 1))
                v.scalar_tensor_tensor(out=Ab[:, 0:nk], in0=pm[0][:, 0:nk], scalar=rz[:, 0:1], in1=pm[1][:, 0:nk],
                                       op0=ALU.mult, op1=ALU.subtract).then_inc(s_A, 1)
                own(s_A)

            def da_norm(n):
                dve.wait_ge(s_ro, n + 1)
                if n:
                    filled(dve, ("oaT", n - 1))
                release(v.tensor_scalar(onb, bank(6)[:, 0:P], rso, None, ALU.mult), ("pv", n))
                read(("pv", n))

            def blocks(a, lv):
                return a.rearrange("p (g b) -> p g b", b=128 >> lv)

            def part_of(a, lv, second):
                half = 64 >> lv
                b = blocks(a, lv)
                return b[:, :, half:2 * half] if second else b[:, :, 0:half]

            def sub(h, lv):
                half = 64 >> lv
                e = E[lv % 2]
                shape = [P, NT * 64 // half, half]
                f, b = blocks(bb[:, 0, :], lv), blocks(bb[:, 1, :], lv)
                rf = f[:, :, half - 1:half].broadcast_to(shape)
                rb = b[:, :, half:half + 1].broadcast_to(shape)
                link(v.tensor_tensor(part_of(e[:, 0, :], lv, 1), f[:, :, half:2 * half], rf, ALU.subtract))
                link(v.tensor_tensor(part_of(e[:, 0, :], lv, 0), rf, f[:, :, 0:half], ALU.subtract))
                link(v.tensor_tensor(part_of(e[:, 1, :], lv, 0), b[:, :, 0:half], rb, ALU.subtract))
                v.tensor_tensor(part_of(e[:, 1, :], lv, 1), rb, b[:, :, half:2 * half], ALU.subtract).then_inc(s_sub, 1)
                own(s_sub)

            def place(h, lv):
                nb, half = 1 << lv, 64 >> lv
                for d in range(2):
                    filled(dve, ("lev", h, lv, d))
                    out = attn.rearrange("p (c g b) -> p c g b", c=NT, g=nb)
                    out = out[:, :, :, half:2 * half] if d == 0 else out[:, :, :, 0:half]
                    msk = masks[:, d, lv, :].rearrange("p (c g j) -> p c g j", c=1, g=nb).broadcast_to([P, NT, nb, half])
                    src = bank(4 + d)[:, 0:320].rearrange("p (c g j) -> p c g j", c=NT, g=nb)
                    release(v.copy_predicated(out, msk.bitcast(I32), src), ("lev", h, lv, d))
                    read(("lev", h, lv, d))

            dve.wait_ge(s_small, 16 * NSM)
            link(v.tensor_tensor(lbs, lbl[:, :, 0, :], lbl[:, :, 1, :], ALU.max))
            link(v.tensor_tensor(lbt[:, :, 0, :], lbl[:, :, 0, :], lbs, ALU.subtract))
            v.tensor_tensor(lbt[:, :, 1, :], lbl[:, :, 1, :], lbs, ALU.subtract).then_inc(s_lbt, 1)
            own(s_lbt)
            v4 = lamv.rearrange("p (a b) e -> p a b e", b=2)
            link(v.tensor_tensor(lamp, v4[:, :, 0, :], v4[:, :, 1, :], ALU.mult))
            v.tensor_reduce(lam[:, 0:2], lamp, AX_X, ALU.add).then_inc(s_lame, 1)
            own(s_lame)
            norm_x(0)
            norm_x(1)

            for n, st in enumerate(STEPS):
                for key in before[n]:
                    lo(key)
                k = st[0]
                if k == "mod" and st[1] not in LATE:
                    j = st[1]
                    filled(dve, ("modcol", j))
                    src = bank(5)[:, 0:8].rearrange("p (q c) -> p q c", c=2)
                    release(v.tensor_tensor(modc[:, 4 * j:4 * j + 4, :], src, bcol[:, 4 * j:4 * j + 4].unsqueeze(2).broadcast_to([P, 4, 2]),
                                            ALU.add), ("modcol", j))
                    read(("modcol", j))
                    if j in (3, 9):
                        dve.wait_ge(free[2], USE[("modcol", j)][2])
                        a_, n_, q0 = (A1, n1c, 8) if j == 3 else (A2, n2c, 32)
                        link(v.scalar_tensor_tensor(out=a_, in0=modc[:, q0:q0 + 8, :], scalar=1.0,
                                                    in1=n_.unsqueeze(2).broadcast_to([P, 8, 2]), op0=ALU.add, op1=ALU.mult))
                elif k == "xT":
                    i = st[1]
                    c = min(i, 1)
                    filled(dve, ("xT", i))
                    if i:
                        dve.wait_ge(s_hh, i)
                        dve.wait_ge(s_hl, i)
                    release(v.tensor_tensor(hf, pair(3).rearrange("p (k t) -> p k t", k=KD), A1[:, :, c:c + 1].broadcast_to([P, KD, P]),
                                            ALU.mult), ("xT", i))
                    read(("xT", i))
                    dve.wait_ge(free[3], USE[("xT", i)][2])
                    v.tensor_tensor(hf, hf, modc[:, 0:8, c:c + 1].broadcast_to([P, KD, P]), ALU.add).then_inc(s_hf, 1)
                    own(s_hf)
                    if i + 2 < NT:
                        norm_x(i + 2)
                    dve.wait_ge(s_hh, i + 1)
                    v.tensor_tensor(act_lo[:, :, P * i:P * i + P], hf, act_hi[:, :, P * i:P * i + P].bitcast(F32),
                                    ALU.subtract).then_inc(s_hl, 1)
                    own(s_hl)
                elif k == "tok" and st[2] == 1 and st[1] < 2:
                    g = st[1]
                    for i in range(NT + 1):
                        if i < NT:
                            sum_q(g, i)
                        if i:
                            norm_q(g, i - 1)
                elif k == "da":
                    n_ = st[1]
                    if n_ + 1 < NI:
                        da_max(n_ + 1)
                    if n_ == -1:
                        dve.wait_ge(s_lame, 2)
                        link(v.scalar_tensor_tensor(out=lam[:, 0:1], in0=lam[:, 2:3], scalar=LAM_INIT, in1=lam[:, 3:4],
                                                    op0=ALU.add, op1=ALU.subtract))
                        v.tensor_scalar(subln8, subln, 1.0 - LAM_INIT, None, ALU.mult).then_inc(s_tbl, 1)
                        own(s_tbl)
                        dve.wait_ge(s_lbe, 1)
                        link(v.tensor_tensor(lbs, lbt[:, :, 0, :], lbt[:, :, 1, :], ALU.add))
                        link(v.reciprocal(lbs, lbs))
                        link(v.tensor_tensor(lb, lbt[:, :, 0, :], lbs, ALU.mult))
                        link(v.tensor_scalar(oml, lb, -1.0, 1.0, ALU.mult, ALU.add))
                    if 0 <= n_ < NI:
                        da_comb(n_)
                    if n_ >= 1:
                        da_norm(n_ - 1)
                elif k == "f":
                    h, d = st[1], st[2]
                    dve.wait_ge(free[d], USE[st][2])
                    link(v.tensor_scalar(Fb[:, d, :], Fb[:, d, :], oml[:, d, h:h + 1], lb[:, d, h:h + 1], ALU.mult, ALU.add))
                elif k == "q":
                    h = st[1]
                    if h == 0:
                        dve.wait_ge(s_nv, 16)
                        link(v.memset(KS, 0.0))
                    v.tensor_scalar(Kb, Fb, -1.0, 1.0, ALU.mult, ALU.add).then_inc(s_f, 1)
                    own(s_f)
                    dve.wait_ge(s_ln, h + 1)
                    link(v.tensor_tensor_scan(bb[:, 0, :], reset, Fb[:, 0, :], 0.0, ALU.mult, ALU.add))
                    v.tensor_tensor_scan(bb[:, 1, ::-1], reset, Fb[:, 1, ::-1], 0.0, ALU.mult, ALU.add).then_inc(s_scan, 1)
                    own(s_scan)
                elif k == "diag":
                    h = st[1]
                    dve.wait_ge(s_scan, h + 1)
                    dve.wait_ge(s_f, h + 1)
                    v.tensor_tensor(QC.rearrange("p d t -> p (d t)"), Kb[:, 0, :], Kb[:, 1, :], ALU.add).then_inc(s_ksum, 1)
                    own(s_ksum)
                    sub(h, 0)
                    filled(dve, st)
                    release(v.tensor_tensor(attn.rearrange("p (c t) -> p c t", c=NT), pair(3)[:, 0:T].rearrange("p (c t) -> p c t", c=NT),
                                            ident.unsqueeze(1).broadcast_to([P, NT, P]), ALU.mult), st)
                    read(st)
                elif k == "lev":
                    h, lv = st[1], st[2]
                    if lv + 1 < LEVELS:
                        sub(h, lv + 1)
                    dve.wait_ge(s_e, LEVELS * h + lv + 1)
                    if lv:
                        filled(dve, ("lev", h, lv - 1, 1))
                    half = 64 >> lv
                    e = E[lv % 2]
                    for d in range(2):
                        qs = 1 - d
                        link(v.tensor_tensor(QC[:, d, :].rearrange("p (g j) -> p g j", j=half), part_of(qh, lv, qs), part_of(e[:, d, :], lv, qs), ALU.mult))
                        ins = v.tensor_tensor(part_of(KS[:, d, :], lv, 1 - qs), part_of(Kb[:, d, :], lv, 1 - qs),
                                              part_of(e[:, d, :], lv, 1 - qs), ALU.mult)
                        if d == 0:
                            link(ins)
                    ins.then_inc(s_qk, 1)
                    own(s_qk)
                    if lv == 0:
                        dve.wait_ge(free[3], USE[("diag", h)][2])
                    else:
                        place(h, lv - 1)
                    if lv == LEVELS - 1:
                        place(h, lv)
                elif k == "tail":
                    h = st[1]
                    b4 = bb.rearrange("p d (c t) -> p d c t", c=NT)
                    e4 = E[0].rearrange("p d (c t) -> p d c t", c=NT)
                    link(v.tensor_tensor(e4[:, 0], b4[:, 0, :, 127:128].broadcast_to([P, NT, P]), b4[:, 0], ALU.subtract))
                    v.tensor_tensor(e4[:, 1], b4[:, 1, :, 0:1].broadcast_to([P, NT, P]), b4[:, 1], ALU.subtract).then_inc(s_ebl, 1)
                    own(s_ebl)
                    dve.wait_ge(free[2], USE[("lev", h, LEVELS - 1, 1)][2])
                    dve.wait_ge(s_ebl2, h + 1)
                    v.tensor_tensor(KS, Kb, E[0], ALU.mult).then_inc(s_ksb, 1)
                    own(s_ksb)
                    dve.wait_ge(s_eb, h + 1)
                    dve.wait_ge(s_st0, 32)
                    v.tensor_tensor(QB[:, :, P:T], qh[:, P:T].unsqueeze(1).broadcast_to([P, 2, NLAT]), E[1][:, :, P:T], ALU.mult).then_inc(s_qb, 1)
                    own(s_qb)
                    if h:
                        dve.wait_ge(s_st, 16 * h)
                    for d in range(2):
                        filled(dve, ("U", h, d))
                        U = bank(4 + d).rearrange("p (s e) -> p s e", s=4)
                        v.tensor_copy(SO[:, d, :], U[:, 0, :]).then_inc(s_so, 1)
                        own(s_so)
                        for j in range(3):
                            c = 1 + j if d == 0 else 4 - j
                            at = P * c + (P - 1 if d == 0 else 0)
                            old = state0[:, d, h, :] if j == 0 else SC[:, d, j - 1, :]
                            ins = v.scalar_tensor_tensor(out=SC[:, d, j, :], in0=old, scalar=E[1][:, d, at:at + 1], in1=U[:, 1 + j, :],
                                                         op0=ALU.mult, op1=ALU.add)
                            if j < 2:
                                link(ins)
                        release(ins, ("U", h, d))
                        read(("U", h, d))
                    dve.wait_ge(s_sq5, h + 1)
                    v.tensor_reduce(ss5, sq5.rearrange("p (c e) -> p c e", c=NT), AX_X, ALU.add).then_inc(s_rd5, 1)
                    own(s_rd5)
                    dve.wait_ge(s_r5, h + 1)
                    g3 = og.rearrange("p (c e) -> p c e", c=NT)
                    release(v.tensor_tensor(g3, pair(3)[:, 0:T].rearrange("p (c e) -> p c e", c=NT),
                                            rs5.unsqueeze(2).broadcast_to([P, NT, P]), ALU.mult), ("o", h))
                    read(("o", h))
                    dve.wait_ge(free[3], USE[("o", h)][2])
                    v.tensor_tensor(g3, g3, sg[:, h], ALU.mult).then_inc(s_og, 1)
                    own(s_og)
                elif k == "mrg":
                    c = st[1]
                    if c == 0:
                        for b, o in enumerate((oh, oa)):
                            dve.wait_ge(s_oth, b + 1)
                            v.tensor_tensor(act_lo[:, 4 * b:4 * b + 4, :], o, act_hi[:, 4 * b:4 * b + 4, :].bitcast(F32),
                                            ALU.subtract).then_inc(s_otl, 1)
                            own(s_otl)
                        dve.wait_ge(s_otl, 2)
                        dve.wait_ge(s_st, 16 * H)
                    if c:
                        dve.wait_ge(s_mg, c)
                    filled(dve, ("mx", c))
                    release(v.tensor_tensor(halves(mt[0]), as2(pair(USE[("mx", c)][0])), halves(gate[:, c, :]), ALU.mult), ("mx", c))
                    read(("mx", c))
                    filled(dve, ("my", c))
                    release(v.tensor_tensor(halves(mt[1]), as2(pair(USE[("my", c)][0])), halves(gate[:, 8 + c, :]), ALU.mult), ("my", c))
                    read(("my", c))
                    for b in ("mx", "my"):
                        dve.wait_ge(free[USE[(b, c)][0]], USE[(b, c)][2])
                    v.tensor_tensor(mg[:, c, :], mt[0], mt[1], ALU.add).then_inc(s_mg, 1)
                    own(s_mg)
                    if c == 7:
                        for b in range(2):
                            dve.wait_ge(s_mgh, b + 1)
                            v.tensor_tensor(act_lo[:, 4 * b:4 * b + 4, :], mg[:, 4 * b:4 * b + 4, :],
                                            act_hi[:, 4 * b:4 * b + 4, :].bitcast(F32), ALU.subtract).then_inc(s_mgl, 1)
                            own(s_mgl)
                elif k == "out" and st[2] == 1:
                    nh = st[1]
                    if nh == 0:
                        dve.wait_ge(s_x1in, 16 * (NT + 1))
                        dve.wait_ge(free[2], USE[("g1", 5, 1)][2])
                    for i in range(NT):
                        filled(dve, ("out", nh, i))
                        y = yt[i % 2]
                        release(v.tensor_tensor(y, bank(i), G1[:, min(i, 1), 512 * nh:512 * nh + 512], ALU.mult), ("out", nh, i))
                        read(("out", nh, i))
                        dve.wait_ge(free[i // 2], USE[("out", nh, i)][2])
                        xx = x1[:, i, 512 * nh:512 * nh + 512]
                        v.tensor_tensor(xx, xx, y, ALU.add).then_inc(s_x1, 1)
                        own(s_x1)
                elif k == "h2T":
                    i = st[1]
                    c = min(i, 1)
                    if i == 0:
                        norm_x2(0)
                        norm_x2(1)
                    filled(dve, ("h2T", i))
                    release(v.tensor_tensor(h2, pair(3).rearrange("p (k t) -> p k t", k=KD), A2[:, :, c:c + 1].broadcast_to([P, KD, P]),
                                            ALU.mult), ("h2T", i))
                    read(("h2T", i))
                    dve.wait_ge(free[3], USE[("h2T", i)][2])
                    v.tensor_tensor(h2, h2, modc[:, 24:32, c:c + 1].broadcast_to([P, KD, P]), ALU.add).then_inc(s_h2, 1)
                    own(s_h2)
                    if i + 2 < NT:
                        norm_x2(i + 2)
                    filled(dve, ("rt", i))
                    link(v.tensor_reduce(rmx, bank(4)[:, 0:NE], AX_X, ALU.max))
                    v.tensor_scalar(rnm, rmx, -1.0, None, ALU.mult).then_inc(s_rm, 1)
                    own(s_rm)
                    dve.wait_ge(free[2], USE[("rt", i)][2])
                    link(v.reciprocal(rrz, rzz))
                    v.tensor_scalar(aff, aff, rrz, None, ALU.mult).then_inc(s_aff, 1)
                    own(s_aff)
                elif k == "top":
                    dve.wait_ge(free[2], USE[("affT", NT - 1)][2])
                    link(v.tensor_copy(wlat[0:NE, :], affT[0:NE, P:T]))
                    link(v.tensor_copy(wctx[0:NE, :], affT[0:NE, 0:P]))
                    for work, rounds, at in ((wlat, CAP_LAT // 8, 0), (wctx, CAP_CTX // 8, CAP_LAT)):
                        w = work[0:NE, :]
                        for r in range(rounds):
                            m8 = vals[0:NE, at + 8 * r:at + 8 * r + 8]
                            link(v.max(m8, w))
                            link(v.max_index(idxu[0:NE, at + 8 * r:at + 8 * r + 8], m8, w))
                            link(v.match_replace(w, m8, w, -1.0))
                    link(v.tensor_copy(idxf[0:NE, 0:CAP], idxu[0:NE, 0:CAP]))
                    v.tensor_scalar(idxf[0:NE, 0:CAP_LAT], idxf[0:NE, 0:CAP_LAT], float(NCTX), None, ALU.add).then_inc(s_gi, 1)
                    own(s_gi)
                    for dst, src in ((A2f, A2), (B2f, modc[:, 24:32, :])):
                        link(v.tensor_copy(dst[:, :, 0:CAP_LAT], src[:, :, 1:2].broadcast_to([P, KD, CAP_LAT])))
                        link(v.tensor_copy(dst[:, :, CAP_LAT:CAP], src[:, :, 0:1].broadcast_to([P, KD, CAP_CTX])))
                    filled(dve, ("gi",))
                    v.tensor_copy(gT[0:CAP, :], pair(3)[0:CAP, 0:NE]).then_inc(s_gt, 1)
                    own(s_gt)
                    v.tensor_copy(iT[0:CAP, :], pair(3)[0:CAP, NE:2 * NE]).then_inc(s_gt, 1)
                    own(s_gt)

            def elo(sl, ready, slot):
                dve.wait_ge(s_eh, ready)
                v.tensor_tensor(Wl[sl], eraw[slot], Wh[sl].bitcast(F32), ALU.subtract).then_inc(s_el, 1)

            def xmod(e):
                dve.wait_ge(s_xgT, e + 1)
                v.tensor_tensor(xgt3, xpsum, A2f, ALU.mult).then_inc(s_xgm, 1)
                dve.wait_ge(s_xgm, e + 1)
                v.tensor_tensor(xgt3, xgt3, B2f, ALU.add).then_inc(s_xgf, 1)
                dve.wait_ge(s_xgf, e + 1)

            def xlo(e):
                dve.wait_ge(s_xgh, e + 1)
                v.tensor_tensor(xl, xgt3, xh.bitcast(F32), ALU.subtract).then_inc(s_xgl, 1)

            def hidden(e, up_made):
                dve.wait_ge(s_silu, e + 1)
                dve.wait_ge(s_eu, up_made)
                v.tensor_tensor(aa[0:CAP, :], aa[0:CAP, :], pair(1)[0:CAP, :], ALU.mult).then_inc(s_a, 1)

            def alo(e):
                dve.wait_ge(s_ahi, e + 1)
                v.tensor_tensor(al, xpsum, ah.bitcast(F32), ALU.subtract).then_inc(s_alo, 1)

            def yout(e, first=False):
                dve.wait_ge(s_eu, min(e * 12 + 20, 12 * NE) if isinstance(e, int) else e * 12 + 20)
                if not first:
                    dve.wait_ge(s_scat, 16 * e)
                v.scalar_tensor_tensor(out=ye[0:CAP, :], in0=pair(2)[0:CAP, :], scalar=gT[0:CAP, bass.ds(e, 1)], in1=G2[0:CAP, :],
                                       op0=ALU.mult, op1=ALU.mult).then_inc(s_y, 1)

            def body(e, first=False, second=False, last=False):
                for j in range(12):
                    elo((j + 2) % NHL, e * 12 + (j - 3), (j + 2) % NRE)
                    if j == 0:
                        alo(e - 1)
                    if j == 1 and not first:
                        yout(e - 2, first=second)
                    if j == 8 and not last:
                        xmod(e + 1)
                    if j == 9:
                        if not last:
                            xlo(e + 1)
                        hidden(e, e * 12 + 4)

            dve.wait_ge(s_gt, 1)
            xmod(0)
            xlo(0)
            for n in range(8):
                elo(n % NHL, n + 1, n % NRE)
            xmod(1)
            xlo(1)
            hidden(0, 8)
            body(1, first=True)
            body(2, second=True)
            with dve.Fori(3, NE - 1) as e:
                body(e)
            body(NE - 1, last=True)
            elo(188 % NHL, 189, 188 % NRE)
            alo(NE - 1)
            elo(189 % NHL, 190, 189 % NRE)
            yout(NE - 2)
            elo(190 % NHL, 191, 190 % NRE)
            elo(191 % NHL, 192, 191 % NRE)
            yout(NE - 1)

        @block.tensor
        def _(pe):
            t = nc.tensor

            def mm3(out, s, m, start, stop):
                (sh, sl), (mh, ml) = s, m
                t.matmul(out, sh, mh, start=start, stop=False)
                t.matmul(out, sh, ml, start=False, stop=False)
                return t.matmul(out, sl, mh, start=False, stop=stop)

            def both(key, k):
                a, b = hl(key)
                return [w[:, 0:width(key)].rearrange("p (k n) -> p k n", k=k) for w in (a, b)]

            def rows_group(kind, g, s):
                key = (kind, g, s)
                pe.wait_ge(s_lo, SPLITNO[key] + 1)
                wh, wl = both(key, 4)
                for i in range(NT):
                    if s == 0:
                        begin(pe, (kind, g, i))
                    for kk in range(4):
                        kt = 4 * s + kk
                        tok = slice(P * i, P * i + P)
                        ins = mm3(bank(i), (act_hi[:, kt, tok], act_lo[:, kt, tok]), (wh[:, kk, :], wl[:, kk, :]), kt == 0, kt == 7)
                    if s == 1:
                        wrote(ins, (kind, g, i))
                if s == 0:
                    ins.then_inc(s_wused, 1)

            def columns(pr, wh, wl, a0, nk):
                for b in range(2):
                    tok = slice(320 * b, 320 * b + 320)
                    for kk in range(nk):
                        ins = mm3(bank(2 * pr + b)[:, 0:320], (wh[:, kk, :], wl[:, kk, :]),
                                  (act_hi[:, a0 + kk, tok], act_lo[:, a0 + kk, tok]), kk == 0, kk == nk - 1)
                return ins

            def scores(n):
                h, i = ITER[n]
                for m in range(2):
                    r = slice(64 * m, 64 * m + 64)
                    begin(pe, ("s", n, m))
                    q = qT[r, h, P * i:P * i + P]
                    if i == 0:
                        ins = t.matmul(pair(m)[:, 0:P], q, kT[r, h, 0:P], start=True, stop=True)
                    else:
                        t.matmul(pair(m)[:, 0:512], q, kT[r, h, P:T], start=True, stop=True)
                        ins = t.matmul(pair(m)[:, 512:640], q, ckT[r, h, :], start=True, stop=True)
                    wrote(ins, ("s", n, m))

            pe.wait_ge(s_small, 16 * NSM)
            for n, st in enumerate(STEPS):
                k = st[0]
                if k == "mod":
                    j = st[1]
                    if j == 0:
                        pe.wait_ge(s_cond, 1)
                    begin(pe, ("modrow", j))
                    for s in range(2):
                        landed(pe, ("mod", j, s))
                        w = rawv(("mod", j, s)).rearrange("p (k n) -> p k n", k=4)
                        for kk in range(4):
                            kt = 4 * s + kk
                            ins = t.matmul(bank(4)[0:2, :], cond[:, kt, :], w[:, kk, :], start=kt == 0, stop=kt == 7)
                        if s == 0:
                            ins.then_inc(s_rused, 1)
                    wrote(ins, ("modrow", j))
                    if j not in LATE:
                        begin(pe, ("modcol", j))
                        for q in range(4):
                            ins = t.transpose(bank(5)[:, 2 * q:2 * q + 2], mrow[0:2, P * q:P * q + P], ident[0:2, 0:2])
                        wrote(ins, ("modcol", j))
                    else:
                        pe.wait_ge(s_brow, 16 * (LATE.index(j) + 1))
                        for w_ in ((0, 1) if j < 6 else (2,)):
                            key = ("g1", j, w_) if j < 6 else ("g2", j)
                            begin(pe, key)
                            t.matmul(bank(4), sel[0:2, w_, :], mrow[0:2, :], start=True, stop=False)
                            wrote(t.matmul(bank(4), sel[0:1, 0, :], brow[0:1, :], start=False, stop=True), key)
                elif k == "xT":
                    i = st[1]
                    pe.wait_ge(s_xn, i + 1)
                    begin(pe, ("xT", i))
                    for q in range(KD):
                        ins = t.transpose(pair(3)[:, P * q:P * q + P], xt[i % 2][:, P * q:P * q + P], ident)
                    wrote(ins, ("xT", i))
                elif k == "split":
                    pe.wait_ge(s_hl, NT)
                elif k in ("tok", "out"):
                    if st == ("out", 0, 0):
                        pe.wait_ge(s_mgl, 2)
                    rows_group(*st)
                elif k == "qkT":
                    g = st[1]
                    for i in range(NT):
                        pe.wait_ge(s_qr, 5 * g + i + 1)
                        begin(pe, ("qkT", g, i))
                        for h in range(H):
                            ins = t.transpose(pair(3)[:, P * h:P * h + P], yq[g][:, i, P * h:P * h + P], ident)
                        wrote(ins, ("qkT", g, i))
                elif k == "da":
                    n_ = st[1]
                    if n_ == -1:
                        pe.wait_ge(free[3], USE[("qkT", 1, NT - 1)][2])
                    if n_ + 1 < NI:
                        scores(n_ + 1)
                    if 0 <= n_ < NI:
                        h, i = ITER[n_]
                        nt = NT if i else 1
                        pe.wait_ge(s_A, n_ + 1)
                        begin(pe, ("AT", n_))
                        for j in range(nt):
                            ins = t.transpose(pair(2)[:, P * j:P * j + P], Ab[:, P * j:P * j + P], ident)
                        wrote(ins, ("AT", n_))
                    if n_ >= 1:
                        begin(pe, ("oaT", n_ - 1))
                        wrote(t.transpose(bank(7)[:, 0:P], onb, ident), ("oaT", n_ - 1))
                    if 0 <= n_ < NI:
                        begin(pe, ("pv", n_))
                        pe.wait_ge(free[2], USE[("AT", n_)][2])
                        for j in range(nt):
                            hs = slice(P * h, P * h + P)
                            vals_ = vd[:, 0, hs] if i == 0 else (vd[:, 1 + j, hs] if j < 4 else cv[:, hs])
                            ins = t.matmul(bank(6)[:, 0:P], ATs[:, P * j:P * j + P], vals_, start=j == 0, stop=j == nt - 1)
                        wrote(ins, ("pv", n_))
                elif k == "f":
                    h, d = st[1], st[2]
                    key = ("f", h)
                    pe.wait_ge(s_lo, SPLITNO[key] + 1)
                    wh, wl = (w[:, 1024 * d:1024 * d + 1024].rearrange("p (k n) -> p k n", k=8) for w in hl(key))
                    begin(pe, st)
                    wrote(columns(d, wh, wl, 0, 8), st)
                elif k == "q":
                    pe.wait_ge(s_lo, SPLITNO[st] + 1)
                    wh, wl = both(st, 8)
                    begin(pe, st)
                    wrote(columns(0, wh, wl, 0, 8), st)
                elif k == "diag":
                    h = st[1]
                    pe.wait_ge(s_ksum, h + 1)
                    begin(pe, st)
                    kk = QC.rearrange("p d t -> p (d t)")
                    for c in range(NT):
                        tok = slice(P * c, P * c + P)
                        ins = t.matmul(pair(3)[:, tok], kk[:, tok], qh[:, tok], start=True, stop=True)
                    wrote(ins, st)
                elif k == "lev":
                    h, lv = st[1], st[2]
                    pe.wait_ge(s_qk, LEVELS * h + lv + 1)
                    for d in range(2):
                        begin(pe, (*st, d))
                        for c in range(NT):
                            ins = t.matmul(bank(4 + d)[:, 64 * c:64 * c + 64], KS[:, d, P * c:P * c + P], QC[:, d, 64 * c:64 * c + 64],
                                           start=True, stop=True)
                        wrote(ins, (*st, d))
                elif k == "tail":
                    h = st[1]
                    pe.wait_ge(s_ksb, h + 1)
                    for d in range(2):
                        begin(pe, ("kT", h, d))
                        for c in range(NT):
                            ins = t.transpose(pair(3)[:, P * c:P * c + P], KS[:, d, P * c:P * c + P], ident)
                        wrote(ins, ("kT", h, d))
                    hs = slice(P * h, P * h + P)
                    for d in range(2):
                        begin(pe, ("U", h, d))
                        pe.wait_ge(free[3], USE[("kT", h, d)][2])
                        for s, c in enumerate((0, 1, 2, 3) if d == 0 else (0, 4, 3, 2)):
                            ins = t.matmul(bank(4 + d)[:, P * s:P * s + P], E[0][:, d, P * c:P * c + P], v_hg[:, c, hs], start=True, stop=True)
                        wrote(ins, ("U", h, d))
                    begin(pe, ("o", h))
                    pe.wait_ge(s_qb, h + 1)
                    pe.wait_ge(free[2], USE[("U", h, 1)][2])
                    for c in range(NT):
                        tok = slice(P * c, P * c + P)
                        ins = t.matmul(pair(3)[:, tok], attn[:, tok], v_hg[:, c, hs], start=True, stop=c == 0)
                        if c:
                            for d in range(2):
                                j = c - 1 if d == 0 else 4 - c
                                S = state0[:, d, h, :] if j == 0 else SC[:, d, j - 1, :]
                                ins = t.matmul(pair(3)[:, tok], QB[:, d, tok], S, start=False, stop=d == 1)
                    wrote(ins, ("o", h))
                    pe.wait_ge(s_og, h + 1)
                    begin(pe, ("oT", h))
                    for c in range(NT):
                        ins = t.transpose(pair(3)[:, P * c:P * c + P], og[:, P * c:P * c + P], ident)
                    wrote(ins, ("oT", h))
                elif k == "gl":
                    c = st[1]
                    key = ("gl", c // 2)
                    pe.wait_ge(s_lo, SPLITNO[key] + 1)
                    wh, wl = (w[:, :, P * (c % 2):P * (c % 2) + P] for w in both(key, 8))
                    begin(pe, st)
                    wrote(columns(c % 2, wh, wl, 0, 8), st)
                elif k == "mrg":
                    c = st[1]
                    if c == 0:
                        pe.wait_ge(s_otl, 2)
                    for b in range(2):
                        key = ("br", b, c // 4)
                        pe.wait_ge(s_lo, SPLITNO[key] + 1)
                        wh, wl = (w[:, :, P * (c % 4):P * (c % 4) + P] for w in both(key, 4))
                        u = ("mx" if b == 0 else "my", c)
                        begin(pe, u)
                        wrote(columns(USE[u][0], wh, wl, 4 * b, 4), u)
                elif k == "h2T":
                    i = st[1]
                    pe.wait_ge(s_xn2, i + 1)
                    begin(pe, ("h2T", i))
                    for q in range(KD):
                        ins = t.transpose(pair(3)[:, P * q:P * q + P], xn2[i % 2][:, P * q:P * q + P], ident)
                    wrote(ins, ("h2T", i))
                    pe.wait_ge(s_h2, i + 1)
                    begin(pe, ("rt", i))
                    for kt in range(KD):
                        ins = t.matmul(bank(4)[:, 0:NE], h2[:, kt, :], router[:, kt, :], start=kt == 0, stop=kt == KD - 1)
                    wrote(ins, ("rt", i))
                    pe.wait_ge(s_aff, i + 1)
                    begin(pe, ("affT", i))
                    wrote(t.transpose(bank(4)[0:NE, 0:P], aff, ident), ("affT", i))
                elif k == "top":
                    pe.wait_ge(s_gi, 1)
                    begin(pe, ("gi",))
                    t.transpose(pair(3)[0:CAP, 0:NE], vals[0:NE, 0:CAP], ident[0:NE, 0:NE])
                    wrote(t.transpose(pair(3)[0:CAP, NE:2 * NE], idxf[0:NE, 0:CAP], ident[0:NE, 0:NE]), ("gi",))

            def turn_x(e, first=False):
                pe.wait_ge(s_gath, (e + 1) * 16)
                for q in range(KD):
                    ins = t.transpose(pair(3)[:, P * q:P * q + CAP], xg[0:CAP, P * q:P * q + P], ident[0:CAP, 0:CAP])
                ins.then_inc(s_xgT, 1)

            def piece_mm(pr, ready, sl, hi_, lo_, j):
                pe.wait_ge(s_el, ready)
                wh, wl = (w[sl].rearrange("p (k n) -> p k n", k=2) for w in (Wh, Wl))
                for kk in range(2):
                    kt = 2 * j + kk
                    for b in range(2):
                        cs = slice(512 * b, 512 * b + 512)
                        ins = mm3(bank(2 * pr + b)[0:CAP, :], (hi_[:, kt, :], lo_[:, kt, :]), (wh[:, kk, cs], wl[:, kk, cs]), kt == 0, kt == 7)
                ins.then_inc(s_eu, 1)

            def turn_a(e):
                pe.wait_ge(s_a, e + 1)
                for q in range(KD):
                    ins = t.transpose(pair(3)[:, P * q:P * q + CAP], aa[0:CAP, P * q:P * q + P], ident[0:CAP, 0:CAP])
                ins.then_inc(s_aT, 1)

            def body(e, first=False, last=False):
                for j in range(12):
                    m, q = j // 4, j % 4
                    if j == 0:
                        pe.wait_ge(s_silu, e)
                    if j == 4:
                        pe.wait_ge(s_a, e)
                    if j == 8:
                        if not last:
                            pe.wait_ge(s_alo, e)
                            turn_x(e + 1)
                        pe.wait_ge(s_alo, e)
                        if not first:
                            pe.wait_ge(s_y, e - 1)
                    hi_, lo_ = (xh, xl) if m < 2 else (ah, al)
                    if j == 0:
                        pe.wait_ge(s_xgl, e + 1)
                    piece_mm(m, e * 12 + (j - 3), (j + 2) % NHL, hi_, lo_, q)
                if not last:
                    pe.wait_ge(s_xgm, e + 2)
                turn_a(e)

            turn_x(0)
            pe.wait_ge(s_xgl, 1)
            for n in range(8):
                piece_mm(n // 4, n + 1, n % NHL, xh, xl, n % 4)
            pe.wait_ge(s_xgm, 1)
            turn_x(1)
            pe.wait_ge(s_xgm, 2)
            turn_a(0)
            body(1, first=True)
            with pe.Fori(2, NE - 1) as e:
                body(e)
            body(NE - 1, last=True)
            pe.wait_ge(s_alo, NE)
            pe.wait_ge(s_y, NE - 1)
            for q in range(4):
                piece_mm(2, 189 + q, (188 + q) % NHL, ah, al, q)


_INS = ['x_prompt', 'x_sample', 'cache_v', 'state_hgrn', 'w_mod', 'b_mod', 'w_in', 'diff_lambda', 'w_branch_hgrn', 'w_branch_attn', 'w_out', 'router_w', 'w_exp_gate', 'w_exp_up', 'w_exp_down']
_OUTS = [((1, 128, 1024), 'float32'), ((1, 512, 1024), 'float32'), ((1, 1, 128, 4, 2, 64), 'float32'),
         ((1, 1, 128, 4, 128), 'float32'), ((1, 1, 2, 4, 128, 128), 'float32')]


def tables():
    import numpy as np
    c = np.zeros((P, K_N), np.float32)
    c[:, K_ID:K_ID + P] = np.eye(P)
    s = np.arange(P)
    m = np.zeros((P, 2, LEVELS, 64), np.float32)
    for lv in range(LEVELS):
        half = 64 >> lv
        for j in range(64):
            same = s // (2 * half) == j // half
            second = (s % (2 * half)) >= half
            m[:, 0, lv, j] = same & ~second
            m[:, 1, lv, j] = same & second
    c[:, K_MASK:K_MASK + 14 * 64] = m.reshape(P, -1)
    c[:, K_RESET:K_RESET + T] = (np.arange(T) % P != 0)
    f = np.float32(10000.0) ** (-np.arange(16, dtype=np.float32) / np.float32(16))
    tok = np.arange(NLAT)
    ang = np.stack([(tok // 64).astype(np.float32)[:, None] * f, (tok % 64).astype(np.float32)[:, None] * f], 1)
    co, si = np.cos(ang), np.sin(ang)
    co = np.stack([co, co], 2).reshape(4, P, 64)
    si = np.stack([-si, si], 2).reshape(4, P, 64)
    c[:, K_COS:K_COS + 256] = co.transpose(1, 0, 2).reshape(P, 256)
    c[:, K_SIN:K_SIN + 256] = si.transpose(1, 0, 2).reshape(P, 256)
    c[0, K_SEL:K_SEL + 128] = 1
    c[1, K_SEL + 128:K_SEL + 256] = 1
    c[1, K_SEL + 256:K_SEL + 256 + CAP_LAT] = 1
    c[0, K_SEL + 256 + CAP_LAT:K_SEL + 256 + CAP] = 1
    return c


def columns_of(x):
    import numpy as np

    def by_p(a, k):
        return np.moveaxis(a.reshape(-1, k, P), 2, 0)

    parts = [by_p(x["norm1_w"], 8), by_p(x["norm2_w"], 8),
             np.stack([by_p(x["c_ctx"], 8)[:, 0], by_p(x["c"], 8)[:, 0]], 2),
             by_p(x["b_mod"], 48), by_p(x["b_gate"], 16), x["hgrn_norm_w"][0].T, x["diff_subln_w"].T,
             by_p(x["hgrn_lb_logits"], 4), np.broadcast_to(x["qk_norm_w"].reshape(1, 128), (P, 128))]
    return np.ascontiguousarray(np.concatenate([a.reshape(P, -1) for a in parts], 1))


def kernel(**inputs):
    import numpy as _np
    import concourse.bacc as _bacc
    from concourse import mybir as _mybir
    from concourse.bass_utils import run_bass_kernel_spmd as _run

    nc = _bacc.Bacc("TRN2", target_bir_lowering=False, num_devices=1)
    arrays, A = {}, {}
    for name in _INS:
        a = _np.ascontiguousarray(inputs[name])
        arrays[f"in_{name}_dram"] = a
        A[name] = nc.dram_tensor(f"in_{name}_dram", a.shape, _mybir.dt.from_np(a.dtype), kind="ExternalInput").ap()
    x = {n: _np.asarray(a) for n, a in inputs.items()}
    laid = {"const": tables(), "cols": columns_of(x),
            "ckT": _np.ascontiguousarray(x["cache_k"].reshape(NPAST, H, 2 * DQK).transpose(2, 1, 0).reshape(P, H * NPAST))}
    for name, a in laid.items():
        arrays[name + "_dram"] = a
        A[name] = nc.dram_tensor(name + "_dram", a.shape, F32, kind="ExternalInput").ap()
    outs = []
    for i, (shape, dtype) in enumerate(_OUTS):
        dt = _mybir.dt.from_np(_np.dtype(dtype))
        outs.append(nc.dram_tensor(f"out_{i}_dram", shape, dt, kind="ExternalOutput").ap())
    fused_step(nc, A, outs)
    r = _run(nc, [arrays], core_ids=[0])
    return tuple(r.results[0][f"out_{i}_dram"] for i in range(len(_OUTS)))
```

```python
from contextlib import ExitStack

import concourse.bass as bass
from concourse import mybir

F32 = mybir.dt.float32
F32R = mybir.dt.float32r
U32 = mybir.dt.uint32
I32 = mybir.dt.int32
ALU = mybir.AluOpType
ACT = mybir.ActivationFunctionType
AX_X = mybir.AxisListType.X

P = 128
D = 1024
KD = D // P
NCTX, NLAT, NPAST = 128, 512, 128
T = NCTX + NLAT
NT = T // P
H = 4
DQK = 64
NE = 16
CAP_LAT, CAP_CTX = 2 * NLAT // NE, 2 * NCTX // NE
CAP = CAP_LAT + CAP_CTX
EPS = 1e-6
SCALE = DQK ** -0.5
LAM_INIT = 0.2
LEVELS = 7
C_HQ, C_FF, C_FB, C_HI, C_HG, C_DQ, C_DK, C_DV, C_GL = (512 * i for i in range(9))
TOK = [C_DQ, C_DK, C_DV, C_HI, C_HG]
K_ID, K_MASK, K_RESET, K_SEL, K_COS, K_SIN = 0, 128, 128 + 14 * 64, 1664, 2048, 2304
K_N = K_SIN + 256
K_COLS = 245


def fused_step(nc, A, outs):
    y_prompt, y_sample, new_k, new_v, new_state = outs
    xn_rows = nc.dram_tensor("xn_rows", (T, D), F32, kind="Internal").ap()
    y_rows = nc.dram_tensor("y_rows", (T, D), F32, kind="Internal").ap()

    w_in, w_mod = A["w_in"][0], A["w_mod"][0]
    x_tile = [A["x_prompt"][0]] + [A["x_sample"][0, i * P:(i + 1) * P, :] for i in range(4)]

    with ExitStack() as ctx:
        def sem(name):
            return ctx.enter_context(nc.semaphore(name))

        N_ARENA = 30680
        arena = ctx.enter_context(nc.sbuf_tensor("arena", [P, N_ARENA], F32))[:, :]
        top = [0]

        def take(n):
            a = arena[:, top[0]:top[0] + n]
            top[0] += n
            assert top[0] <= N_ARENA, (top[0], N_ARENA)
            return a

        NRAW = 3
        raw = [take(2048) for _ in range(NRAW)]
        o_x = top[0]
        X = take(12544)
        o_vso = top[0]
        v_hg = take(2560).rearrange("p (i n) -> p i n", i=NT)
        sg_flat = take(2560)
        sg = sg_flat.rearrange("p (h i n) -> p h i n", h=H, i=NT)
        oh = sg_flat.rearrange("p (h t) -> p h t", h=H)
        oa = take(2560).rearrange("p (h t) -> p h t", h=H)
        mg = arena[:, o_vso + 2560:o_vso + 7680].rearrange("p (c t) -> p c t", c=8)
        const = take(K_N)
        o_st = top[0] - 512
        take(512)
        cols = take(K_COLS)
        ident = const[:, K_ID:K_ID + 128]
        masks = const[:, K_MASK:K_MASK + 14 * 64].rearrange("p (d l j) -> p d l j", d=2, l=LEVELS)
        reset = const[:, K_RESET:K_RESET + T]
        cosT = const[:, K_COS:K_COS + 256].rearrange("p (i e) -> p i e", i=4)
        sinT = const[:, K_SIN:K_SIN + 256].rearrange("p (i e) -> p i e", i=4)
        sel = const[:, K_SEL:K_SEL + 384].rearrange("p (w n) -> p w n", w=3)
        at = [0]

        def col(n):
            at[0] += n
            return cols[:, at[0] - n:at[0]]

        n1c, n2c = col(8), col(8)
        condf = col(16).rearrange("p (k c) -> p k c", c=2)
        bcol = col(48)
        bgate = col(16)
        hnw = col(4)
        subln = col(1)
        lbl = col(16).rearrange("p (d l h) -> p d l h", d=2, l=2)
        qkw = col(128).rearrange("p (m e) -> p m e", m=2)
        cond = take(16).rearrange("p (k c) -> p k c", c=2)
        subln8 = take(1)
        lb = take(8).rearrange("p (d h) -> p d h", d=2)
        oml = take(8).rearrange("p (d h) -> p d h", d=2)
        lbt = take(16).rearrange("p (d l h) -> p d l h", d=2, l=2)
        lbs = take(8).rearrange("p (d h) -> p d h", d=2)
        lam = take(4)
        modc = take(96).rearrange("p (q c) -> p q c", c=2)
        A1 = take(16).rearrange("p (k c) -> p k c", c=2)
        A2 = take(16).rearrange("p (k c) -> p k c", c=2)
        ss1, rs1 = take(5), take(5)
        ss2, rs2 = take(5), take(5)
        ssq, rsq = take(80).rearrange("p (n e) -> p n e", e=8), take(80).rearrange("p (n e) -> p n e", e=8)
        negh = take(8)
        mx = take(2)
        nm, zz = [take(2) for _ in range(2)], [take(2) for _ in range(2)]
        rz = [take(2) for _ in range(3)]
        mix = take(1)
        sso, rso = take(1), take(1)
        ss5, rs5 = take(5), take(5)
        rmx, rzz, rrz = take(5), take(5), take(5)
        mrow = take(512)
        state0 = arena[:, o_st:o_st + 1024].rearrange("p (d h e) -> p d h e", d=2, h=H)

        def part(base, n):
            return X[:, base:base + n]

        xt = [part(0, 1024), part(1024, 1024)]
        sq1 = part(2048, 1024)
        hf = part(3072, 1024).rearrange("p (k t) -> p k t", k=KD)
        qT = part(0, 2560).rearrange("p (h t) -> p h t", h=H)
        kT = part(2560, 2560).rearrange("p (h t) -> p h t", h=H)
        vd = part(5120, 2560).rearrange("p (i n) -> p i n", i=NT)
        cv = part(8192, 512)
        ckT = part(8704, 512).rearrange("p (h t) -> p h t", h=H)
        pm = [[part(9216, 640), part(9856, 640)], [part(10496, 640), part(11904, 640)]]
        ATs = part(11136, 640)
        onb = part(11776, 128)
        lamv = part(7680, 256).rearrange("p (r e) -> p r e", r=4)
        lamp = part(7936, 128).rearrange("p (r e) -> p r e", r=2)
        sqq = part(9216, 512)
        qn = part(9728, 512)
        zr = part(10752, 512)
        QB = part(11264, 1280).rearrange("p (d t) -> p d t", d=2)
        sqo = part(8064, 128)
        Fb = part(0, 1280).rearrange("p (d t) -> p d t", d=2)
        Kb = part(1280, 1280).rearrange("p (d t) -> p d t", d=2)
        qh = part(2560, 640)
        bb = part(3200, 1280).rearrange("p (d t) -> p d t", d=2)
        E = [part(4480, 1280).rearrange("p (d t) -> p d t", d=2), part(5760, 1280).rearrange("p (d t) -> p d t", d=2)]
        KS = [part(b, 1280).rearrange("p (d t) -> p d t", d=2) for b in (7040, 11264)]
        QC = [part(b, 640).rearrange("p (d t) -> p d t", d=2) for b in (8320, 10624)]
        attn = part(8960, 640)
        SC = part(9600, 768).rearrange("p (d j e) -> p d j e", d=2, j=3)
        SO = part(10368, 256).rearrange("p (d e) -> p d e", d=2)
        og = part(10624, 640)
        sq5 = og
        gate = part(0, 10240).rearrange("p (c t) -> p c t", c=16)
        mt = [part(10240, 640), part(10880, 640)]
        x1 = part(0, 5120).rearrange("p (i n) -> p i n", i=NT)
        yt = [part(5120, 512), part(5632, 512)]
        xn2 = [part(6144, 1024), part(7168, 1024)]
        sq2 = part(8192, 1024)
        h2 = [part(b, 1024).rearrange("p (k t) -> p k t", k=KD) for b in (9216, 8192)]
        aff = part(11648, NT * NE).rearrange("p (i e) -> p i e", i=NT)
        brow11 = part(11776, 512)
        affT = part(10256, 640)
        wlat = part(10896, 512)
        router = part(11520, 128).rearrange("p (k e) -> p k e", k=8)
        G1 = arena[:, o_vso:o_vso + 2048].rearrange("p (c n) -> p c n", c=2)
        m0 = o_vso + 2560
        wctx = arena[:, m0:m0 + 128]
        vals = arena[:, m0 + 128:m0 + 208]
        idxf = arena[:, m0 + 208:m0 + 288]
        idxu = arena[:, m0 + 288:m0 + 368].bitcast(U32)
        gT = arena[:, m0 + 368:m0 + 384]
        iT = arena[:, m0 + 384:m0 + 400].bitcast(U32)
        gcur = arena[:, m0 + 400:m0 + 402]
        icur = arena[:, m0 + 402:m0 + 404].bitcast(U32)
        iscat = arena[:, m0 + 404:m0 + 405].bitcast(U32)
        A2f = arena[:, m0 + 512:m0 + 1152].rearrange("p (k t) -> p k t", k=KD)
        B2f = arena[:, m0 + 1152:m0 + 1792].rearrange("p (k t) -> p k t", k=KD)
        G2 = arena[:, m0 + 1792:m0 + 2816]
        xg = arena[:, m0 + 2816:m0 + 3840]
        aa = arena[:, m0 + 3840:m0 + 4864]
        assert 4864 <= 5120
        G2s = G2
        NRE = 6
        eraw = [part(0, 2048), part(2048, 2048), part(4096, 2048)] + raw
        ye = part(6144, 1024)
        xgt = part(7168, 640)
        xgt3 = xgt.rearrange("p (k t) -> p k t", k=KD)

        NHL = 3
        Wh = [ctx.enter_context(nc.sbuf_tensor(f"w_hi{s}", [P, 2048], F32R))[:, :] for s in range(NHL)]
        Wl = [ctx.enter_context(nc.sbuf_tensor(f"w_lo{s}", [P, 2048], F32R))[:, :] for s in range(NHL)]
        act_hi = ctx.enter_context(nc.sbuf_tensor("act_hi", [P, KD, T], F32R))[:, :, :]
        act_lo = ctx.enter_context(nc.sbuf_tensor("act_lo", [P, KD, T], F32R))[:, :, :]
        brow = arena[:, o_vso + 2048:o_vso + 2560]
        yq = [v_hg, arena[:, o_vso + 2560:o_vso + 5120].rearrange("p (i n) -> p i n", i=NT)]
        kctx = yq[1][:, 0, :]
        xh, xl = (w[:, 0, :].rearrange("p (k t) -> p k t", k=KD) for w in (act_hi, act_lo))
        ah, al = (w[:, 1, :].rearrange("p (k t) -> p k t", k=KD) for w in (act_hi, act_lo))

        PS = ctx.enter_context(nc.psum_tensor("ps", [P, 4096], F32))[:, :]

        def pair(n):
            return PS[:, 1024 * n:1024 * n + 1024]

        def bank(b):
            return PS[:, 512 * b:512 * b + 512]

        xpsum = pair(3).rearrange("p (k t) -> p k t", k=KD)[:, :, 0:CAP]

        def as2(a):
            return a.rearrange("p (b t) -> p b t", b=2)[:, :, 0:320]

        def halves(a):
            return a.rearrange("p (b t) -> p b t", b=2)

        full = [sem(f"psum_full{n}") for n in range(4)]
        free = [sem(f"psum_free{n}") for n in range(4)]
        ledger = [0] * 4
        USE = {}

        def use(key, pr, units=2, beside=0):
            assert key not in USE
            USE[key] = (pr, ledger[pr] - beside, ledger[pr] + units, units)
            ledger[pr] += units

        PIECES, RAWNO, SPLITNO, RELEASE = [], {}, {}, {}

        def piece(key, srcs, split=True):
            RAWNO[key] = len(PIECES)
            if split:
                SPLITNO[key] = len(SPLITNO)
            PIECES.append((key, srcs, split))

        def rows(w, c0, n, k0, k):
            return w[k0 * P:(k0 + k) * P, c0:c0 + n].rearrange("(k p) n -> p k n", p=P)

        def mod_pieces(j):
            for s in range(2):
                piece(("mod", j, s), [(0, 512, 4, rows(w_mod, 512 * j, 512, 4 * s, 4))], split=False)

        ITER = [(h, i) for h in range(H) for i in range(NT)]
        NI = len(ITER)
        STEPS = []
        for j in range(4):
            mod_pieces(j)
            STEPS.append(("mod", j))
        for i in range(NT):
            STEPS.append(("xT", i))
        STEPS.append(("split",))
        for g in range(5):
            for s in range(2):
                piece(("tok", g, s), [(0, 512, 4, rows(w_in, TOK[g], 512, 4 * s, 4))])
                STEPS.append(("tok", g, s))
                if s == 0 and g in (1, 2):
                    STEPS.append(("qkT", g - 1))
        STEPS.append(("da", -1))
        for n in range(NI + 2):
            STEPS.append(("da", n))

        def head_pieces(h):
            piece(("f", h), [(0, 128, 8, rows(w_in, C_FF + 128 * h, 128, 0, 8)), (1024, 128, 8, rows(w_in, C_FB + 128 * h, 128, 0, 8))])
            piece(("q", h), [(0, 128, 8, rows(w_in, C_HQ + 128 * h, 128, 0, 8))])

        def gl_piece(c):
            piece(("gl", c), [(0, 256, 8, rows(w_in, C_GL + 256 * c, 256, 0, 8))])

        head_pieces(0)
        head_pieces(1)
        mod_pieces(6)
        head_pieces(2)
        mod_pieces(7)
        head_pieces(3)
        mod_pieces(8)
        gl_piece(0)
        gl_piece(1)
        mod_pieces(9)
        gl_piece(2)
        gl_piece(3)
        mod_pieces(4)
        gl_piece(4)
        gl_piece(5)
        mod_pieces(5)
        gl_piece(6)
        gl_piece(7)
        def projections(h):
            return [("pf", h, 0, 0), ("pf", h, 0, 1), ("pf", h, 1, 0), ("pf", h, 1, 1), ("pq", h, 0), ("pq", h, 1)]

        STEPS += projections(0)[0:2] + [("f", 0, 0)] + projections(0)[2:4] + [("f", 0, 1)] + projections(0)[4:6]
        STEPS += [("fa", 0, 0), ("fa", 0, 1), ("q", 0)]
        STEPS += [("pre", 0), ("diag", 0)]
        for h in range(H):
            todo = projections(h + 1) if h + 1 < H else []
            for lv in range(LEVELS):
                STEPS.append(("lev", h, lv))
                if todo:
                    STEPS.append(todo.pop(0))
                if h + 1 < H and lv in (3, 5):
                    STEPS.append(("f", h + 1, lv // 2 - 1))
                if h + 1 < H and lv in (4, 6):
                    STEPS.append(("fa", h + 1, lv // 2 - 2))
                if lv == 0:
                    if h:
                        STEPS += [("sq", h - 1), ("oT", h - 1)]
                    STEPS.append(("dattn", h))
            STEPS.append(("prep", h))
            if h + 1 < H:
                STEPS.append(("q", h + 1))
            STEPS += [("mod", 6 + h), ("states", h), ("o", h)]
            if h + 1 < H:
                STEPS += [("pre", h + 1), ("diag", h + 1)]
            else:
                STEPS += [("sq", h), ("oT", h)]
        LATE = [4, 5, 10, 11]
        for c in range(8):
            STEPS.append(("gl", 2 * c))
            STEPS.append(("gl", 2 * c + 1))
            if c in (1, 3):
                STEPS.append(("mod", LATE[c // 2]))
        for c in range(8):
            if c % 4 == 0:
                for b, w in enumerate((A["w_branch_hgrn"][0], A["w_branch_attn"][0])):
                    piece(("br", b, c // 4), [(0, 512, 4, rows(w, 512 * (c // 4), 512, 0, 4))])
            STEPS.append(("mrg", c))
        for n in range(2):
            for s in range(2):
                piece(("out", n, s), [(0, 512, 4, rows(A["w_out"][0], 512 * n, 512, 4 * s, 4))])
                STEPS.append(("out", n, s))
        for i in range(NT + 1):
            STEPS.append(("h2T", i))
        for j in LATE[2:]:
            mod_pieces(j)
            STEPS.append(("mod", j))
        STEPS.append(("top",))

        def modpair(j):
            return 3 if 6 <= j < 10 else 2

        for st in STEPS:
            k = st[0]
            if k == "mod":
                j = st[1]
                use(("modrow", j), modpair(j))
                if j in LATE:
                    if j < 6:
                        use(("g1", j, 0), 2)
                        use(("g1", j, 1), 2)
                    else:
                        use(("g2", j), 2)
                else:
                    use(("modcol", j), modpair(j))
            elif k == "xT":
                use(("xT", st[1]), 3)
            elif k in ("tok", "out") and st[2] == 0:
                for i in range(NT):
                    use((k, st[1], i), i // 2, 1, i % 2)
            elif k == "qkT":
                for i in range(NT):
                    use(("qkT", st[1], i), 3)
            elif k == "da":
                n = st[1]
                if n + 1 < NI:
                    use(("s", n + 1, 0), 0)
                    use(("s", n + 1, 1), 1)
                if 0 <= n < NI:
                    use(("AT", n), 2)
            elif k == "pf" and st[3] == 0:
                use(("f", st[1], st[2]), st[2])
            elif k == "pq" and st[2] == 0:
                use(("q", st[1]), 0)
            elif k == "diag":
                use(st, 1)
            elif k == "lev":
                use((*st, 0), 2 + st[2] % 2, 1)
                use((*st, 1), 2 + st[2] % 2, 1, 1)
            elif k in ("o", "oT"):
                use(st, 3)
            elif k == "states":
                h = st[1]
                use(("kT", h, 0), 3)
                use(("kT", h, 1), 3)
                use(("U", h, 0), 2, 1)
                use(("U", h, 1), 2, 1, 1)
            elif k == "gl":
                use(st, st[1] % 2)
            elif k == "mrg":
                c = st[1]
                use(("mx", c), 2 * (c % 2))
                use(("my", c), 2 * (c % 2) + 1)
            elif k == "h2T":
                if st[1] < NT:
                    use(("h2T", st[1]), 3 if st[1] % 2 == 0 else 1)
                else:
                    use(("rt",), 0)
                    use(("affT",), 1)
            elif k == "top":
                use(("gi",), 3)

        def filled(eng, key):
            eng.wait_ge(full[USE[key][0]], USE[key][2])

        def release(ins, key):
            return ins.then_inc(free[USE[key][0]], USE[key][3])

        def begin(pe, key):
            if USE[key][1]:
                pe.wait_ge(free[USE[key][0]], USE[key][1])

        def wrote(ins, key):
            return ins.then_inc(full[USE[key][0]], USE[key][3])

        s_small = sem("s_small")
        s_late = sem("s_late")
        s_raw = [sem(f"s_raw{s}") for s in range(NRAW)]
        s_hi, s_lo = sem("s_hi"), sem("s_lo")
        s_wused = sem("s_wused")
        s_rused = sem("s_rused")
        s_x = [sem("s_xin0"), sem("s_xin1")]
        s_sq1, s_r1, s_xn, s_hf, s_hh, s_hl = (sem(n) for n in ("s_sq1", "s_r1", "s_xn", "s_hf", "s_hh", "s_hl"))
        s_cond, s_mrow, s_lbe, s_lame = sem("s_cond"), sem("s_mrow"), sem("s_lbe"), sem("s_lame")
        s_neg = sem("s_neg")
        s_pool = sem("s_pool")
        s_v = sem("s_v")
        s_sqq, s_rdq, s_rq, s_qr = sem("s_sqq"), sem("s_rdq"), sem("s_rq"), sem("s_qr")
        s_nm, s_p, s_A, s_AT = sem("s_nm"), sem("s_p"), sem("s_A"), sem("s_AT")
        s_sqo, s_ro = sem("s_sqo"), sem("s_ro")
        s_pv, s_onb, s_oaT, s_oa = sem("s_pv"), sem("s_onb"), sem("s_oaT"), sem("s_oa")
        s_sig, s_f, s_ln, s_sub, s_e, s_qk, s_attn = (sem(n) for n in ("s_sig", "s_f", "s_ln", "s_sub", "s_e", "s_qk", "s_attn"))
        s_qsilu, s_ksum = sem("s_qsilu"), sem("s_ksum")
        s_eb, s_ebl, s_ksb, s_qb, s_S, s_so = (sem(n) for n in ("s_eb", "s_ebl", "s_ksb", "s_qb", "s_S", "s_so"))
        s_sq5, s_rd5, s_r5, s_og, s_tl = sem("s_sq5"), sem("s_rd5"), sem("s_r5"), sem("s_og"), sem("s_tl")
        s_oth, s_otl, s_mgh, s_mgl, s_mg = (sem(n) for n in ("s_oth", "s_otl", "s_mgh", "s_mgl", "s_mg"))
        s_x1in, s_x1, s_sq2, s_r2, s_xn2, s_h2, s_rm, s_re, s_aff = (
            sem(n) for n in ("s_x1in", "s_x1", "s_sq2", "s_r2", "s_xn2", "s_h2", "s_rm", "s_re", "s_aff"))
        s_xrow = [sem("s_xrow0"), sem("s_xrow1")]
        s_gi, s_gt, s_kc = sem("s_gi"), sem("s_gt"), sem("s_kc")
        s_nk, s_nv, s_st, s_yrow, s_yout = (sem(n) for n in ("s_nk", "s_nv", "s_st", "s_yrow", "s_yout"))
        s_st0, s_go = sem("s_st0"), sem("s_go")
        s_brow, s_brow11, s_lbt, s_scan = sem("s_brow"), sem("s_brow11"), sem("s_lbt"), sem("s_scan")
        s_icq, s_xgm, s_rt, s_ebl2, s_tbl = (sem(n) for n in ("s_icq", "s_xgm", "s_rt", "s_ebl2", "s_tbl"))
        s_er = [sem(f"s_er{s}") for s in range(NRE)]
        s_eh, s_el, s_eu = sem("s_eh"), sem("s_el"), sem("s_eu")
        s_icp, s_gath, s_xgT, s_xgf, s_xgh, s_xgl = (sem(n) for n in ("s_icp", "s_gath", "s_xgT", "s_xgf", "s_xgh", "s_xgl"))
        s_gt_e, s_up, s_dn, s_silu, s_a, s_aT, s_afc, s_ahi, s_alo, s_y, s_scat, s_gcp = (sem(n) for n in (
            "s_gt_e", "s_up", "s_dn", "s_silu", "s_a", "s_aT", "s_afc", "s_ahi", "s_alo", "s_y", "s_scat", "s_gcp"))

        rawfill = {}
        count = [0] * NRAW
        for n, (key, srcs, split) in enumerate(PIECES):
            count[n % NRAW] += 16 * len(srcs)
            rawfill[key] = count[n % NRAW]
        modno = {}
        for key, srcs, split in PIECES:
            if not split:
                modno[key] = len(modno) + 1

        used, nw, nr = {}, 0, 0
        for key, _, _ in PIECES:
            k = key[0]
            if k == "mod":
                if key[2] == 0:
                    nr += 1
                    used[key] = (s_rused, nr)
                else:
                    used[key] = (full[modpair(key[1])], USE[("modrow", key[1])][2])
            elif k in ("tok", "out"):
                if key[2] == 0:
                    nw += 1
                    used[key] = (s_wused, nw)
                else:
                    used[key] = (full[2], USE[(k, key[1], 4)][2])
            elif k == "f":
                used[key] = (full[1], USE[("f", key[1], 1)][2])
            elif k == "q":
                used[key] = (full[0], USE[key][2])
            elif k == "gl":
                used[key] = (full[1], USE[("gl", 2 * key[1] + 1)][2])
            elif k == "br":
                c = 4 * key[2] + 3
                used[key] = (full[USE[("my", c)][0]], USE[("my", c)][2])

        def landed(eng, key):
            eng.wait_ge(s_raw[RAWNO[key] % NRAW], rawfill[key])

        def rawv(key):
            return raw[RAWNO[key] % NRAW]

        def hl(key):
            s = SPLITNO[key] % NHL
            return Wh[s], Wl[s]

        SPLITS = [k for k, _, sp in PIECES if sp]
        AHEAD = 2
        before = {}
        nxt = 0
        for n, st in enumerate(STEPS):
            k = st[0]
            last = None
            ahead = AHEAD
            if k in ("tok", "out"):
                last = SPLITNO[st]
            elif k == "pf" and st[2] == 0 and st[3] == 0:
                last, ahead = SPLITNO[("f", st[1])], 1
            elif k == "pq" and st[2] == 0:
                last, ahead = SPLITNO[("q", st[1])], 1 if st[1] < H - 1 else 0
            elif k == "lev" and st[1] == H - 1 and st[2] in (3, 5):
                last, ahead = SPLITNO[("gl", st[2] // 2 - 1)], 0
            elif k == "gl" and st[1] % 2 == 0:
                last = SPLITNO[("gl", st[1] // 2)]
            elif k == "mrg" and st[1] % 4 == 0:
                last = SPLITNO[("br", 1, st[1] // 4)]
            todo = []
            if last is not None:
                while nxt < len(SPLITS) and nxt <= last + (ahead if k != "mrg" else 1):
                    todo.append(SPLITS[nxt])
                    nxt += 1
            before[n] = todo
        assert nxt == len(SPLITS)

        def width(key):
            return 1024 if key[0] == "q" else 2048

        block = ctx.enter_context(nc.Block())

        @block.sync
        def _(sp):
            small = [
                (const, A["const"]),
                (cols, A["cols"]),
                (lamv, A["diff_lambda"][0].partition_broadcast(P)),
                (ckT.rearrange("p h t -> p (h t)"), A["ckT"]),
                (cv, A["cache_v"][0, 0].rearrange("t h d -> t (h d)")),
            ]
            for dst, src in small[0:2]:
                sp.dma_start(dst, src).then_inc(s_small, 16)

            def load(n):
                key, srcs, split = PIECES[n]
                if n >= NRAW:
                    old = PIECES[n - NRAW][0]
                    if old in SPLITNO:
                        sp.wait_ge(s_lo, SPLITNO[old] + 1)
                    else:
                        sp.wait_ge(*used[old])
                for off, cols, k, src in srcs:
                    dst = raw[n % NRAW][:, off:off + cols * k].rearrange("p (k n) -> p k n", k=k)
                    sp.dma_start(dst, src).then_inc(s_raw[n % NRAW], 16)

            def load_x(i):
                if i >= 2:
                    filled(sp, ("xT", i - 2))
                sp.dma_start(xt[i % 2], x_tile[i]).then_inc(s_x[i % 2], 16)

            def load_brow(j):
                sp.dma_start((brow11 if j == 11 else brow)[0:1, :], A["b_mod"][0:1, 512 * j:512 * j + 512]).then_inc(s_brow11 if j == 11 else s_brow, 16)

            load(0)
            load(1)
            load_x(0)
            load(2)
            load_x(1)
            for dst, src in small[2:]:
                sp.dma_start(dst, src).then_inc(s_late, 16)
            for n in range(3, 8):
                load(n)
            for i in range(2, NT):
                load_x(i)
            out_at = {"nk": RAWNO[("tok", 3, 1)], "nv": RAWNO[("tok", 4, 1)]}
            for n in range(8, len(PIECES) - 1):
                if n == out_at["nk"]:
                    sp.wait_ge(s_qr, 2 * NT)
                    sp.dma_start(new_k[0, 0].rearrange("t h m d -> t (h m d)"), kctx).then_inc(s_nk, 16)
                    for d in range(2):
                        sp.dma_start(state0[:, d], A["state_hgrn"][0, 0, d].rearrange("h k e -> k h e")).then_inc(s_st0, 16)
                if n == out_at["nv"]:
                    sp.wait_ge(free[USE[("tok", 2, 0)][0]], USE[("tok", 2, 0)][2])
                    sp.dma_start(new_v[0, 0].rearrange("t h d -> t (h d)"), vd[:, 0, :]).then_inc(s_nv, 16)
                if n in (RAWNO[("gl", 2)], RAWNO[("gl", 4)]):
                    filled(sp, ("o", H - 1) if n == RAWNO[("gl", 2)] else ("g1", 4, 1))
                    load_brow(4 if n == RAWNO[("gl", 2)] else 5)
                load(n)
                if n == RAWNO[("out", 0, 0)]:
                    sp.wait_ge(s_mg, 8)
                    for i in range(NT):
                        sp.dma_start(x1[:, i, :], x_tile[i]).then_inc(s_x1in, 16)
                    sp.dma_start(router, A["router_w"][0].rearrange("(k p) e -> p k e", p=P)).then_inc(s_x1in, 16)
            filled(sp, ("g1", 5, 1))
            load_brow(10)
            load_brow(11)
            for i in range(NT):
                sp.wait_ge(s_x1, NT + i + 1)
                sp.dma_start(y_rows[i * P:(i + 1) * P, :], x1[:, i, :]).then_inc(s_yrow, 16)
            for i in range(NT):
                sp.wait_ge(s_xn2, i + 1)
                sp.dma_start(xn_rows[i * P:(i + 1) * P, :], xn2[i % 2]).then_inc(s_xrow[i % 2], 16)
            load(len(PIECES) - 1)

            wg, wu, wd = (A[n][0] for n in ("w_exp_gate", "w_exp_up", "w_exp_down"))

            def epiece(w, e, k, slot):
                src = w[bass.ds(e, 1), bass.ts(k, 2 * P), :].rearrange("a (k p) n -> p (a k) n", p=P)
                sp.dma_start(eraw[slot].rearrange("p (k n) -> p k n", k=2), src).then_inc(s_er[slot], 16)

            sp.wait_ge(s_yrow, 16 * NT)
            sp.wait_ge(s_xn2, NT)
            sp.wait_ge(s_sq2, NT)
            for n in range(8):
                if n == NRE - NRAW:
                    sp.wait_ge(s_lo, len(SPLITS))
                    sp.wait_ge(*used[("mod", LATE[-1], 1)])
                if n >= NRE:
                    sp.wait_ge(s_el, n - NRE + 1)
                epiece(wg if n < 4 else wu, 0, n % 4, n % NRE)
            with sp.Fori(1, NE) as e:
                for j in range(12):
                    sp.wait_ge(s_el, e * 12 + (j - 4 - NRE + 1))
                    if j < 4:
                        epiece(wg, e, j, (j + 2) % NRE)
                    elif j < 8:
                        epiece(wu, e, j - 4, (j + 2) % NRE)
                    else:
                        epiece(wd, e - 1, j - 8, (j + 2) % NRE)
            for j in range(4):
                sp.wait_ge(s_el, 188 + j - NRE + 1)
                epiece(wd, NE - 1, j, (188 + j) % NRE)
            sp.wait_ge(s_scat, 16 * NE)
            sp.dma_start(y_prompt[0], y_rows[0:NCTX, :]).then_inc(s_yout, 16)
            sp.dma_start(y_sample[0], y_rows[NCTX:T, :]).then_inc(s_yout, 16)
            sp.wait_ge(s_nk, 16)
            sp.wait_ge(s_nv, 16)
            sp.wait_ge(s_st, 16 * H)
            sp.wait_ge(s_yout, 32)

        @block.gpsimd
        def _(pool):
            g = nc.gpsimd
            chain = [0]

            def link(ins):
                chain[0] += 1
                ins.then_inc(s_pool, 1)
                pool.wait_ge(s_pool, chain[0])

            g.memset(negh, -0.5).then_inc(s_neg, 1)
            pool.wait_ge(s_neg, 1)

            def rroot(out, ss, n, sig, w):
                link(g.tensor_scalar(out, ss, 1.0 / n, EPS, ALU.mult, ALU.add))
                g.tensor_tensor(out, out, negh[:, 0:w], ALU.pow).then_inc(sig, 1)

            for i in range(NT):
                pool.wait_ge(s_sq1, i + 1)
                rroot(rs1[:, i:i + 1], ss1[:, i:i + 1], D, s_r1, 1)
            for n in range(2 * NT):
                pool.wait_ge(s_rdq, n + 1)
                rroot(rsq[:, n, :], ssq[:, n, :], DQK, s_rq, 8)
            for n in range(NI):
                pool.wait_ge(s_sqo, n + 1)
                if n:
                    pool.wait_ge(s_onb, n)
                rroot(rso, sso, P, s_ro, 1)
            for h in range(H):
                pool.wait_ge(s_so, 2 * (h + 1))
                pool.dma_start(new_state[0, 0, :, h].rearrange("d k e -> k d e"), SO).then_inc(s_st, 16)
                pool.wait_ge(s_rd5, h + 1)
                rroot(rs5, ss5, P, s_r5, 5)
            for i in range(NT):
                pool.wait_ge(s_sq2, i + 1)
                rroot(rs2[:, i:i + 1], ss2[:, i:i + 1], D, s_r2, 1)

            pool.wait_ge(s_gt, 2)
            for s in range(2):
                pool.wait_ge(s_xrow[s], 16 * (3 - s))
            pool.wait_ge(s_yrow, 16 * NT)

            def fetch():
                g.indirect_dma_start(out=xg[0:CAP, :], out_offset=None, in_=xn_rows,
                                     in_offset=bass.IndirectOffsetOnAxis(ap=icur[0:CAP, 0:1], axis=0)).then_inc(s_gath, 16)

            def gather(e):
                pool.wait_ge(s_xgT, e)
                g.tensor_copy(icur[0:CAP, 0:1], iT[0:CAP, bass.ds(e, 1)]).then_inc(s_icp, 1)
                pool.wait_ge(s_icp, e + 1)
                pool.sem_inc(s_go, 1)
                fetch()

            def scatter(e):
                g.tensor_copy(iscat[0:CAP, 0:1], iT[0:CAP, bass.ds(e, 1)]).then_inc(s_icq, 1)
                pool.wait_ge(s_icq, e + 1)
                pool.wait_ge(s_y, e + 1)
                pool.sem_inc(s_go, 1)
                g.indirect_dma_start(out=y_rows, out_offset=bass.IndirectOffsetOnAxis(ap=iscat[0:CAP, 0:1], axis=0),
                                     in_=ye[0:CAP, :], in_offset=None, compute_op=ALU.add).then_inc(s_scat, 16)
                pool.wait_ge(s_scat, 16 * e + 16)

            g.tensor_copy(icur[0:CAP, 0:1], iT[0:CAP, 0:1]).then_inc(s_icp, 1)
            pool.wait_ge(s_icp, 1)
            fetch()
            gather(1)
            gather(2)
            with pool.Fori(2, NE - 1) as e:
                gather(e + 1)
                scatter(e - 2)
            for e in range(NE - 3, NE):
                scatter(e)

        @block.scalar
        def _(act):
            a = nc.scalar
            act.wait_ge(s_small, 32)
            a.activation(cond, condf, ACT.Silu).then_inc(s_cond, 1)

            def square_x(t):
                act.wait_ge(s_x[t % 2], 16 * (t // 2 + 1))
                if t:
                    act.wait_ge(s_sq1, t)
                a.activation(sq1, xt[t % 2], ACT.Square, accum_out=ss1[:, t:t + 1]).then_inc(s_sq1, 1)

            square_x(0)
            square_x(1)
            nsplit = [0]

            def hi(key):
                n, w = SPLITNO[key], width(key)
                landed(act, key)
                if n >= NHL:
                    act.wait_ge(*used[SPLITS[n - NHL]])
                a.activation(hl(key)[0][:, 0:w], rawv(key)[:, 0:w], ACT.Copy).then_inc(s_hi, 1)

            def evac(dst, key, func=ACT.Copy, src=None, **kw):
                filled(act, key)
                release(a.activation(dst, src, func, **kw), key)

            def da_exp(n):
                h, i = ITER[n]
                nk = 640 if i else 128
                act.wait_ge(s_nm, n + 1)
                for m in range(2):
                    filled(act, ("s", n, m))
                    release(a.activation(pm[n % 2][m][:, 0:nk], pair(m)[:, 0:nk], ACT.Exp, scale=SCALE,
                                         bias=nm[n % 2][:, m:m + 1], accum_out=zz[n % 2][:, m:m + 1]), ("s", n, m))

            for n, st in enumerate(STEPS):
                for key in before[n]:
                    hi(key)
                k = st[0]
                if k == "mod":
                    j = st[1]
                    evac(mrow[0:2, :], ("modrow", j), src=bank(2 * modpair(j))[0:2, :])
                    if j in (4, 5):
                        for c in range(2):
                            evac(G1[:, c, 512 * (j - 4):512 * (j - 3)], ("g1", j, c), src=bank(4))
                    if j in (10, 11):
                        act.wait_ge(s_mgl, 8)
                        evac(G2s[0:CAP, 512 * (j - 10):512 * (j - 9)], ("g2", j), src=bank(4)[0:CAP, :])
                elif k == "xT":
                    i = st[1]
                    act.wait_ge(s_hf, i + 1)
                    a.activation(act_hi[:, :, P * i:P * i + P], hf, ACT.Copy).then_inc(s_hh, 1)
                    if i + 2 < NT:
                        square_x(i + 2)
                elif k == "tok" and st[2] == 1:
                    g = st[1]
                    for i in range(NT):
                        key = ("tok", g, i)
                        if g < 2:
                            filled(act, key)
                            if g or i:
                                act.wait_ge(s_rdq, 5 * g + i)
                            a.activation(sqq, bank(i), ACT.Square).then_inc(s_sqq, 1)
                        elif g == 2:
                            evac(vd[:, i, :], key, src=bank(i))
                        elif g == 3:
                            evac(v_hg[:, i, :], key, src=bank(i))
                        else:
                            if i == 0:
                                act.wait_ge(s_nk, 16)
                            evac(sg[:, :, i, :], key, ACT.Silu, src=bank(i).rearrange("p (h n) -> p h n", h=H))
                elif k == "qkT":
                    act.wait_ge(s_hl, NT)
                    for i in range(NT):
                        dst = (qT, kT)[st[1]][:, :, P * i:P * i + P]
                        evac(dst, ("qkT", st[1], i), src=pair(3)[:, 0:512].rearrange("p (h t) -> p h t", h=H))
                elif k == "da":
                    n = st[1]
                    if n == -1:
                        act.wait_ge(s_tbl, 1)
                        act.wait_ge(s_lame, 1)
                        a.activation(lam[:, 2:4], lam[:, 0:2], ACT.Exp).then_inc(s_lame, 1)
                        act.wait_ge(s_lbt, 1)
                        a.activation(lbt, lbt, ACT.Exp).then_inc(s_lbe, 1)
                    if n + 1 < NI:
                        da_exp(n + 1)
                    if 0 <= n - 1 < NI:
                        act.wait_ge(s_pv, n)
                        if n >= 2:
                            act.wait_ge(s_ro, n - 1)
                        a.activation(sqo, bank(6)[:, 0:P], ACT.Square, scale=rz[(n - 1) % 3][:, 0:1], accum_out=sso).then_inc(s_sqo, 1)
                    if 0 <= n < NI:
                        nk = 640 if ITER[n][1] else 128
                        if n:
                            act.wait_ge(s_pv, n)
                        evac(ATs[:, 0:nk], ("AT", n), src=pair(2)[:, 0:nk])
                    if n >= 2:
                        h, i = ITER[n - 2]
                        act.wait_ge(s_oaT, n - 1)
                        a.activation(oa[:, h, P * i:P * i + P], bank(7)[:, 0:P], ACT.Copy, scale=subln8).then_inc(s_oa, 1)
                elif k == "f":
                    h, d = st[1], st[2]
                    if h and d == 0:
                        act.wait_ge(s_scan, h)
                        filled(act, ("diag", h - 1))
                    evac(halves(Fb[:, d, :]), st, ACT.Sigmoid, src=as2(pair(d)))
                elif k == "q":
                    h = st[1]
                    if h:
                        act.wait_ge(s_qb, h)
                    evac(halves(qh), st, ACT.Silu, src=as2(pair(0)))
                    act.wait_ge(s_f, h + 1)
                    a.activation(Fb, Fb, ACT.Ln).then_inc(s_ln, 1)
                elif k == "lev":
                    h, lv = st[1], st[2]
                    act.wait_ge(s_sub, LEVELS * h + lv + 1)
                    a.activation(E[lv % 2], E[lv % 2], ACT.Exp).then_inc(s_e, 1)
                elif k == "prep":
                    h = st[1]
                    act.wait_ge(s_qk, LEVELS * (h + 1))
                    a.activation(E[1], bb, ACT.Exp).then_inc(s_eb, 1)
                    act.wait_ge(s_ebl, h + 1)
                    a.activation(E[0], E[0], ACT.Exp).then_inc(s_ebl2, 1)
                elif k == "states":
                    h = st[1]
                    if h + 1 < H:
                        act.wait_ge(s_scan, h + 2)
                    for d in range(2):
                        evac(Fb[:, d, :], ("kT", h, d), src=pair(3)[:, 0:T])
                elif k == "sq":
                    h = st[1]
                    filled(act, ("o", h))
                    a.activation(sq5, pair(3)[:, 0:T], ACT.Square).then_inc(s_sq5, 1)
                elif k == "oT":
                    h = st[1]
                    evac(oh[:, h, :], ("oT", h), src=pair(3)[:, 0:T], scale=hnw[:, h:h + 1])
                elif k == "gl":
                    c = st[1]
                    if c == 0:
                        act.wait_ge(s_so, 2 * H)
                    evac(halves(gate[:, c, :]), st, ACT.Sigmoid, src=as2(pair(c % 2)), bias=bgate[:, c:c + 1])
                elif k == "mrg":
                    if st[1] == 0:
                        filled(act, ("gl", 15))
                        filled(act, ("gl", 14))
                        for c in range(8):
                            a.activation(act_hi[:, c, :], (oh, oa)[c // 4][:, c % 4, :], ACT.Copy).then_inc(s_oth, 1)
                    if st[1] == 7:
                        filled(act, ("my", 7))
                        filled(act, ("my", 6))
                        act.wait_ge(s_mg, 8)
                        for c in range(8):
                            a.activation(act_hi[:, c, :], mg[:, c, :], ACT.Copy).then_inc(s_mgh, 1)
                elif k == "h2T":
                    if st[1] == 0:
                        for t in range(NT):
                            act.wait_ge(s_x1, NT + t + 1)
                            if t:
                                act.wait_ge(s_sq2, t)
                            a.activation(sq2, x1[:, t, :], ACT.Square, accum_out=ss2[:, t:t + 1]).then_inc(s_sq2, 1)
                    if st[1] == NT:
                        act.wait_ge(s_rm, 1)
                        a.activation(aff, aff, ACT.Exp).then_inc(s_re, 1)
                        evac(affT[0:NE, :], ("affT",), src=pair(1)[0:NE, 0:T])

            def xhi(e):
                act.wait_ge(s_xgf, e + 1)
                a.activation(xh, xgt3, ACT.Copy).then_inc(s_xgh, 1)

            def ahi(e):
                act.wait_ge(s_aT, e + 1)
                a.activation(ah, xpsum, ACT.Copy).then_inc(s_ahi, 1)

            def silu(e):
                act.wait_ge(s_eu, e * 12)
                act.wait_ge(s_aT, e)
                a.activation(aa[0:CAP, :], pair(0)[0:CAP, :], ACT.Silu).then_inc(s_silu, 1)

            def body(e, last=False):
                for j in range(12):
                    ehi_at(e, j)
                    if j == 3:
                        ahi(e - 1)
                    if j == 7:
                        silu(e)
                    if j == 10 and not last:
                        xhi(e + 1)

            def ehi_at(e, j):
                act.wait_ge(s_er[(j + 2) % NRE], (e * 2 + (j - 4) // 6 + 1) * 16)
                act.wait_ge(s_eu, e * 12 + (j - 6))
                a.activation(Wh[(j + 2) % NHL], eraw[(j + 2) % NRE], ACT.Copy).then_inc(s_eh, 1)

            xhi(0)
            for n in range(8):
                act.wait_ge(s_er[n % NRE], 16 * (n // NRE + 1))
                if n >= NHL:
                    act.wait_ge(s_eu, n - 2)
                a.activation(Wh[n % NHL], eraw[n % NRE], ACT.Copy).then_inc(s_eh, 1)
            act.wait_ge(s_eu, 4)
            a.activation(aa[0:CAP, :], pair(0)[0:CAP, :], ACT.Silu).then_inc(s_silu, 1)
            xhi(1)
            body(1)
            with act.Fori(2, NE - 1) as e:
                body(e)
            body(NE - 1, last=True)
            for n in range(188, 192):
                act.wait_ge(s_er[n % NRE], 16 * (n // NRE + 1))
                act.wait_ge(s_eu, n - 2)
                a.activation(Wh[n % NHL], eraw[n % NRE], ACT.Copy).then_inc(s_eh, 1)
                if n == 188:
                    ahi(NE - 1)

        @block.vector
        def _(dve):
            v = nc.vector
            chain = [0]

            def link(ins):
                chain[0] += 1
                ins.then_inc(s_v, 1)
                dve.wait_ge(s_v, chain[0])

            count = {}

            def own(sig):
                count[sig.name] = count.get(sig.name, 0) + 1
                dve.wait_ge(sig, count[sig.name])

            def read(key):
                dve.wait_ge(free[USE[key][0]], USE[key][2])

            def lo(key):
                n, w = SPLITNO[key], width(key)
                dve.wait_ge(s_hi, n + 1)
                h_, l_ = hl(key)
                v.tensor_tensor(l_[:, 0:w], rawv(key)[:, 0:w], h_[:, 0:w].bitcast(F32), ALU.subtract).then_inc(s_lo, 1)

            def norm_x(t):
                dve.wait_ge(s_r1, t + 1)
                v.tensor_scalar(xt[t % 2], xt[t % 2], rs1[:, t:t + 1], None, ALU.mult).then_inc(s_xn, 1)
                own(s_xn)

            def norm_x2(t):
                dve.wait_ge(s_r2, t + 1)
                if t >= 2:
                    dve.wait_ge(s_xrow[t % 2], 16 * (t // 2))
                v.tensor_scalar(xn2[t % 2], x1[:, t, :], rs2[:, t:t + 1], None, ALU.mult).then_inc(s_xn2, 1)
                own(s_xn2)

            def sum_q(g, i):
                dve.wait_ge(s_sqq, 5 * g + i + 1)
                v.tensor_reduce(ssq[:, 5 * g + i, :], sqq.rearrange("p (g e) -> p g e", g=8), AX_X, ALU.add).then_inc(s_rdq, 1)
                own(s_rdq)

            def norm_q(g, i):
                n = 5 * g + i
                dve.wait_ge(s_rq, n + 1)
                q3 = qn.rearrange("p (g e) -> p g e", g=8)
                y = yq[g][:, i, :]
                y3 = y.rearrange("p (g e) -> p g e", g=8)
                w = qkw[:, g:g + 1, :].broadcast_to([P, 8, DQK])
                r = rsq[:, n, :].unsqueeze(2).broadcast_to([P, 8, DQK])
                release(v.tensor_tensor(q3, bank(i).rearrange("p (g e) -> p g e", g=8), r, ALU.mult), ("tok", g, i))
                read(("tok", g, i))
                dve.wait_ge(free[i // 2], USE[("tok", g, i)][2])
                if i == 0:
                    v.tensor_tensor(y3, q3, w, ALU.mult).then_inc(s_qr, 1)
                    own(s_qr)
                    return
                link(v.tensor_tensor(q3, q3, w, ALU.mult))
                cc = cosT[:, i - 1:i, :].broadcast_to([P, 8, DQK])
                link(v.tensor_tensor(y3, q3, cc, ALU.mult))
                q5 = qn.rearrange("p (g a b e) -> p g a b e", g=8, a=2, b=2)
                z5 = zr.rearrange("p (g a b e) -> p g a b e", g=8, a=2, b=2)
                s5 = sinT[:, i - 1, :].rearrange("p (g a b e) -> p g a b e", g=1, a=2, b=2)
                link(v.tensor_tensor(z5[:, :, :, 0, :], q5[:, :, :, 1, :], s5[:, :, :, 0, :].broadcast_to([P, 8, 2, 16]), ALU.mult))
                link(v.tensor_tensor(z5[:, :, :, 1, :], q5[:, :, :, 0, :], s5[:, :, :, 1, :].broadcast_to([P, 8, 2, 16]), ALU.mult))
                v.tensor_tensor(y, y, zr, ALU.add).then_inc(s_qr, 1)
                own(s_qr)

            def da_max(n):
                nk = 640 if ITER[n][1] else 128
                for m in range(2):
                    filled(dve, ("s", n, m))
                    link(v.tensor_reduce(mx[:, m:m + 1], pair(m)[:, 0:nk], AX_X, ALU.max))
                v.tensor_scalar(nm[n % 2], mx, -SCALE, None, ALU.mult).then_inc(s_nm, 1)
                own(s_nm)

            def da_comb(n):
                nk = 640 if ITER[n][1] else 128
                dve.wait_ge(free[1], USE[("s", n, 1)][2])
                dve.wait_ge(free[0], USE[("s", n, 0)][2])
                z, r = zz[n % 2], rz[n % 3]
                link(v.reciprocal(r, z))
                link(v.scalar_tensor_tensor(out=mix, in0=r[:, 1:2], scalar=z[:, 0:1], in1=lam[:, 0:1], op0=ALU.mult, op1=ALU.mult))
                p0, p1 = (q[:, 0:nk] for q in pm[n % 2])
                v.scalar_tensor_tensor(out=p0, in0=p1, scalar=mix, in1=p0, op0=ALU.mult, op1=ALU.add).then_inc(s_A, 1)
                own(s_A)

            def da_norm(n):
                dve.wait_ge(s_ro, n + 1)
                if n:
                    dve.wait_ge(s_oaT, n)
                v.tensor_scalar(onb, bank(6)[:, 0:P], rso, rz[n % 3][:, 0:1], ALU.mult, ALU.mult).then_inc(s_onb, 1)
                own(s_onb)

            def blocks(a, lv):
                return a.rearrange("p (g b) -> p g b", b=128 >> lv)

            def part_of(a, lv, second):
                half = 64 >> lv
                b = blocks(a, lv)
                return b[:, :, half:2 * half] if second else b[:, :, 0:half]

            def sub(h, lv):
                half = 64 >> lv
                e = E[lv % 2]
                shape = [P, NT * 64 // half, half]
                f, b = blocks(bb[:, 0, :], lv), blocks(bb[:, 1, :], lv)
                rf = f[:, :, half - 1:half].broadcast_to(shape)
                rb = b[:, :, half:half + 1].broadcast_to(shape)
                link(v.tensor_tensor(part_of(e[:, 0, :], lv, 1), f[:, :, half:2 * half], rf, ALU.subtract))
                link(v.tensor_tensor(part_of(e[:, 0, :], lv, 0), rf, f[:, :, 0:half], ALU.subtract))
                link(v.tensor_tensor(part_of(e[:, 1, :], lv, 0), b[:, :, 0:half], rb, ALU.subtract))
                v.tensor_tensor(part_of(e[:, 1, :], lv, 1), rb, b[:, :, half:2 * half], ALU.subtract).then_inc(s_sub, 1)
                own(s_sub)

            def place(h, lv):
                nb, half = 1 << lv, 64 >> lv
                for d in range(2):
                    filled(dve, ("lev", h, lv, d))
                    out = attn.rearrange("p (c g b) -> p c g b", c=NT, g=nb)
                    out = out[:, :, :, half:2 * half] if d == 0 else out[:, :, :, 0:half]
                    msk = masks[:, d, lv, :].rearrange("p (c g j) -> p c g j", c=1, g=nb).broadcast_to([P, NT, nb, half])
                    src = bank(4 + 2 * (lv % 2) + d)[:, 0:320].rearrange("p (c g j) -> p c g j", c=NT, g=nb)
                    release(v.copy_predicated(out, msk.bitcast(I32), src), ("lev", h, lv, d))
                    read(("lev", h, lv, d))

            dve.wait_ge(s_small, 32)
            link(v.tensor_tensor(lbs, lbl[:, :, 0, :], lbl[:, :, 1, :], ALU.max))
            link(v.tensor_tensor(lbt[:, :, 0, :], lbl[:, :, 0, :], lbs, ALU.subtract))
            v.tensor_tensor(lbt[:, :, 1, :], lbl[:, :, 1, :], lbs, ALU.subtract).then_inc(s_lbt, 1)
            own(s_lbt)
            norm_x(0)
            norm_x(1)
            dve.wait_ge(s_late, 48)
            v4 = lamv.rearrange("p (a b) e -> p a b e", b=2)
            link(v.tensor_tensor(lamp, v4[:, :, 0, :], v4[:, :, 1, :], ALU.mult))
            v.tensor_reduce(lam[:, 0:2], lamp, AX_X, ALU.add).then_inc(s_lame, 1)
            own(s_lame)

            for n, st in enumerate(STEPS):
                for key in before[n]:
                    lo(key)
                k = st[0]
                if k == "mod" and st[1] not in LATE:
                    j = st[1]
                    filled(dve, ("modcol", j))
                    src = bank(2 * modpair(j) + 1)[:, 0:8].rearrange("p (q c) -> p q c", c=2)
                    release(v.tensor_tensor(modc[:, 4 * j:4 * j + 4, :], src, bcol[:, 4 * j:4 * j + 4].unsqueeze(2).broadcast_to([P, 4, 2]),
                                            ALU.add), ("modcol", j))
                    read(("modcol", j))
                    if j in (3, 9):
                        dve.wait_ge(free[modpair(j)], USE[("modcol", j)][2])
                        a_, n_, q0 = (A1, n1c, 8) if j == 3 else (A2, n2c, 32)
                        link(v.scalar_tensor_tensor(out=a_, in0=modc[:, q0:q0 + 8, :], scalar=1.0,
                                                    in1=n_.unsqueeze(2).broadcast_to([P, 8, 2]), op0=ALU.add, op1=ALU.mult))
                elif k == "xT":
                    i = st[1]
                    c = min(i, 1)
                    filled(dve, ("xT", i))
                    if i:
                        dve.wait_ge(s_hh, i)
                        dve.wait_ge(s_hl, i)
                    release(v.tensor_tensor(hf, pair(3).rearrange("p (k t) -> p k t", k=KD), A1[:, :, c:c + 1].broadcast_to([P, KD, P]),
                                            ALU.mult), ("xT", i))
                    read(("xT", i))
                    dve.wait_ge(free[3], USE[("xT", i)][2])
                    v.tensor_tensor(hf, hf, modc[:, 0:8, c:c + 1].broadcast_to([P, KD, P]), ALU.add).then_inc(s_hf, 1)
                    own(s_hf)
                    if i + 2 < NT:
                        norm_x(i + 2)
                    dve.wait_ge(s_hh, i + 1)
                    v.tensor_tensor(act_lo[:, :, P * i:P * i + P], hf, act_hi[:, :, P * i:P * i + P].bitcast(F32),
                                    ALU.subtract).then_inc(s_hl, 1)
                    own(s_hl)
                elif k == "tok" and st[2] == 1 and st[1] < 2:
                    g = st[1]
                    for i in range(NT + 1):
                        if i < NT:
                            sum_q(g, i)
                        if i:
                            norm_q(g, i - 1)
                elif k == "da":
                    n_ = st[1]
                    if n_ == -1:
                        v.tensor_scalar(subln8, subln, 1.0 - LAM_INIT, None, ALU.mult).then_inc(s_tbl, 1)
                        own(s_tbl)
                        da_max(0)
                        dve.wait_ge(s_lame, 2)
                        link(v.scalar_tensor_tensor(out=lam[:, 0:1], in0=lam[:, 3:4], scalar=LAM_INIT, in1=lam[:, 2:3],
                                                    op0=ALU.subtract, op1=ALU.subtract))
                        dve.wait_ge(s_lbe, 1)
                        link(v.tensor_tensor(lbs, lbt[:, :, 0, :], lbt[:, :, 1, :], ALU.add))
                        link(v.reciprocal(lbs, lbs))
                        link(v.tensor_tensor(lb, lbt[:, :, 0, :], lbs, ALU.mult))
                        link(v.tensor_scalar(oml, lb, -1.0, 1.0, ALU.mult, ALU.add))
                    if 0 <= n_ < NI:
                        da_comb(n_)
                    if n_ >= 2:
                        da_norm(n_ - 2)
                    if 0 <= n_ < NI - 1:
                        da_max(n_ + 1)
                elif k == "fa":
                    h, d = st[1], st[2]
                    dve.wait_ge(free[d], USE[("f", h, d)][2])
                    link(v.tensor_scalar(Fb[:, d, :], Fb[:, d, :], oml[:, d, h:h + 1], lb[:, d, h:h + 1], ALU.mult, ALU.add))
                elif k == "q":
                    h = st[1]
                    if h == 0:
                        dve.wait_ge(s_nv, 16)
                        for b in range(2):
                            link(v.memset(KS[b], 0.0))
                    v.tensor_scalar(Kb, Fb, -1.0, 1.0, ALU.mult, ALU.add).then_inc(s_f, 1)
                    own(s_f)
                    dve.wait_ge(s_ln, h + 1)
                    link(v.tensor_tensor_scan(bb[:, 0, :], reset, Fb[:, 0, :], 0.0, ALU.mult, ALU.add))
                    v.tensor_tensor_scan(bb[:, 1, ::-1], reset, Fb[:, 1, ::-1], 0.0, ALU.mult, ALU.add).then_inc(s_scan, 1)
                    own(s_scan)
                elif k == "pre":
                    h = st[1]
                    if h:
                        filled(dve, ("U", h - 1, 1))
                    v.tensor_tensor(Fb[:, 0, :], Kb[:, 0, :], Kb[:, 1, :], ALU.add).then_inc(s_ksum, 1)
                    own(s_ksum)
                    sub(h, 0)
                elif k == "dattn":
                    key = ("diag", st[1])
                    filled(dve, key)
                    release(v.tensor_tensor(attn.rearrange("p (c t) -> p c t", c=NT), pair(1)[:, 0:T].rearrange("p (c t) -> p c t", c=NT),
                                            ident.unsqueeze(1).broadcast_to([P, NT, P]), ALU.mult), key)
                    read(key)
                elif k == "lev":
                    h, lv = st[1], st[2]
                    if lv + 1 < LEVELS:
                        sub(h, lv + 1)
                    dve.wait_ge(s_e, LEVELS * h + lv + 1)
                    if lv >= 2:
                        filled(dve, ("lev", h, lv - 2, 1))
                    elif lv == 1 and h:
                        filled(dve, ("oT", h - 1))
                    half = 64 >> lv
                    e, ks, qc = E[lv % 2], KS[lv % 2], QC[lv % 2]
                    for d in range(2):
                        qs = 1 - d
                        link(v.tensor_tensor(qc[:, d, :].rearrange("p (g j) -> p g j", j=half), part_of(qh, lv, qs), part_of(e[:, d, :], lv, qs), ALU.mult))
                        ins = v.tensor_tensor(part_of(ks[:, d, :], lv, 1 - qs), part_of(Kb[:, d, :], lv, 1 - qs),
                                              part_of(e[:, d, :], lv, 1 - qs), ALU.mult)
                        if d == 0:
                            link(ins)
                    ins.then_inc(s_qk, 1)
                    own(s_qk)
                    if lv >= 2:
                        place(h, lv - 2)
                elif k == "prep":
                    h = st[1]
                    b4 = bb.rearrange("p d (c t) -> p d c t", c=NT)
                    e4 = E[0].rearrange("p d (c t) -> p d c t", c=NT)
                    link(v.tensor_tensor(e4[:, 0], b4[:, 0, :, 127:128].broadcast_to([P, NT, P]), b4[:, 0], ALU.subtract))
                    v.tensor_tensor(e4[:, 1], b4[:, 1, :, 0:1].broadcast_to([P, NT, P]), b4[:, 1], ALU.subtract).then_inc(s_ebl, 1)
                    own(s_ebl)
                    place(h, LEVELS - 2)
                    place(h, LEVELS - 1)
                    for par in range(2):
                        lv = LEVELS - 2 + par
                        dve.wait_ge(free[2 + lv % 2], USE[("lev", h, lv, 1)][2])
                    dve.wait_ge(s_ebl2, h + 1)
                    v.tensor_tensor(KS[0], Kb, E[0], ALU.mult).then_inc(s_ksb, 1)
                    own(s_ksb)
                    dve.wait_ge(s_eb, h + 1)
                    dve.wait_ge(s_st0, 32)
                    v.tensor_tensor(QB[:, :, P:T], qh[:, P:T].unsqueeze(1).broadcast_to([P, 2, NLAT]), E[1][:, :, P:T], ALU.mult).then_inc(s_qb, 1)
                    own(s_qb)
                elif k == "states":
                    h = st[1]
                    if h:
                        dve.wait_ge(s_st, 16 * h)
                    for d in range(2):
                        filled(dve, ("U", h, d))
                        U = bank(4 + d).rearrange("p (s e) -> p s e", s=4)
                        v.tensor_copy(SO[:, d, :], U[:, 0, :]).then_inc(s_so, 1)
                        own(s_so)
                        for j in range(3):
                            c = 1 + j if d == 0 else 4 - j
                            at = P * c + (P - 1 if d == 0 else 0)
                            old = state0[:, d, h, :] if j == 0 else SC[:, d, j - 1, :]
                            ins = v.scalar_tensor_tensor(out=SC[:, d, j, :], in0=old, scalar=E[1][:, d, at:at + 1], in1=U[:, 1 + j, :],
                                                         op0=ALU.mult, op1=ALU.add)
                            if j < 2:
                                link(ins)
                        release(ins, ("U", h, d))
                        read(("U", h, d))
                elif k == "sq":
                    h = st[1]
                    dve.wait_ge(s_sq5, h + 1)
                    v.tensor_reduce(ss5, sq5.rearrange("p (c e) -> p c e", c=NT), AX_X, ALU.add).then_inc(s_rd5, 1)
                    own(s_rd5)
                    dve.wait_ge(s_r5, h + 1)
                    g3 = og.rearrange("p (c e) -> p c e", c=NT)
                    release(v.tensor_tensor(g3, pair(3)[:, 0:T].rearrange("p (c e) -> p c e", c=NT),
                                            rs5.unsqueeze(2).broadcast_to([P, NT, P]), ALU.mult), ("o", h))
                    read(("o", h))
                    dve.wait_ge(free[3], USE[("o", h)][2])
                    v.tensor_tensor(g3, g3, sg[:, h], ALU.mult).then_inc(s_og, 1)
                    own(s_og)
                elif k == "mrg":
                    c = st[1]
                    if c == 0:
                        for q in range(8):
                            dve.wait_ge(s_oth, q + 1)
                            v.tensor_tensor(act_lo[:, q, :], (oh, oa)[q // 4][:, q % 4, :], act_hi[:, q, :].bitcast(F32),
                                            ALU.subtract).then_inc(s_otl, 1)
                            own(s_otl)
                        dve.wait_ge(s_st, 16 * H)
                    if c:
                        dve.wait_ge(s_mg, c)
                    filled(dve, ("mx", c))
                    release(v.tensor_tensor(halves(mt[0]), as2(pair(USE[("mx", c)][0])), halves(gate[:, c, :]), ALU.mult), ("mx", c))
                    read(("mx", c))
                    filled(dve, ("my", c))
                    release(v.tensor_tensor(halves(mt[1]), as2(pair(USE[("my", c)][0])), halves(gate[:, 8 + c, :]), ALU.mult), ("my", c))
                    read(("my", c))
                    for b in ("mx", "my"):
                        dve.wait_ge(free[USE[(b, c)][0]], USE[(b, c)][2])
                    v.tensor_tensor(mg[:, c, :], mt[0], mt[1], ALU.add).then_inc(s_mg, 1)
                    own(s_mg)
                    if c == 7:
                        for q in range(8):
                            dve.wait_ge(s_mgh, q + 1)
                            v.tensor_tensor(act_lo[:, q, :], mg[:, q, :], act_hi[:, q, :].bitcast(F32),
                                            ALU.subtract).then_inc(s_mgl, 1)
                            own(s_mgl)
                elif k == "out" and st[2] == 1:
                    nh = st[1]
                    if nh == 0:
                        dve.wait_ge(s_x1in, 16 * (NT + 1))
                        dve.wait_ge(free[2], USE[("g1", 5, 1)][2])
                    for i in range(NT):
                        filled(dve, ("out", nh, i))
                        y = yt[i % 2]
                        release(v.tensor_tensor(y, bank(i), G1[:, min(i, 1), 512 * nh:512 * nh + 512], ALU.mult), ("out", nh, i))
                        read(("out", nh, i))
                        dve.wait_ge(free[i // 2], USE[("out", nh, i)][2])
                        xx = x1[:, i, 512 * nh:512 * nh + 512]
                        v.tensor_tensor(xx, xx, y, ALU.add).then_inc(s_x1, 1)
                        own(s_x1)
                elif k == "h2T":
                    i = st[1]
                    c = min(i, 1)
                    if i == 0:
                        norm_x2(0)
                        norm_x2(1)
                    if i < NT:
                        if i >= 2:
                            dve.wait_ge(s_rt, i - 1)
                        if i == 1:
                            dve.wait_ge(s_sq2, NT)
                        h2_, pr = h2[i % 2], USE[("h2T", i)][0]
                        filled(dve, ("h2T", i))
                        release(v.tensor_tensor(h2_, pair(pr).rearrange("p (k t) -> p k t", k=KD), A2[:, :, c:c + 1].broadcast_to([P, KD, P]),
                                                ALU.mult), ("h2T", i))
                        read(("h2T", i))
                        v.tensor_tensor(h2_, h2_, modc[:, 24:32, c:c + 1].broadcast_to([P, KD, P]), ALU.add).then_inc(s_h2, 1)
                        own(s_h2)
                        if i + 2 < NT:
                            norm_x2(i + 2)
                    else:
                        logits = bank(0)[:, 0:NT * NE].rearrange("p (i e) -> p i e", i=NT)
                        filled(dve, ("rt",))
                        link(v.tensor_reduce(rmx, logits, AX_X, ALU.max))
                        v.tensor_tensor(aff, logits, rmx.unsqueeze(2).broadcast_to([P, NT, NE]), ALU.subtract).then_inc(s_rm, 1)
                        own(s_rm)
                        dve.wait_ge(s_re, 1)
                        link(v.tensor_reduce(rzz, aff, AX_X, ALU.add))
                        link(v.reciprocal(rrz, rzz))
                        v.tensor_tensor(aff, aff, rrz.unsqueeze(2).broadcast_to([P, NT, NE]), ALU.mult).then_inc(s_aff, 1)
                        own(s_aff)
                elif k == "top":
                    dve.wait_ge(free[1], USE[("affT",)][2])
                    link(v.tensor_copy(wlat[0:NE, :], affT[0:NE, P:T]))
                    link(v.tensor_copy(wctx[0:NE, :], affT[0:NE, 0:P]))
                    for work, rounds, at in ((wlat, CAP_LAT // 8, 0), (wctx, CAP_CTX // 8, CAP_LAT)):
                        w = work[0:NE, :]
                        for r in range(rounds):
                            m8 = vals[0:NE, at + 8 * r:at + 8 * r + 8]
                            link(v.max(m8, w))
                            link(v.max_index(idxu[0:NE, at + 8 * r:at + 8 * r + 8], m8, w))
                            link(v.match_replace(w, m8, w, -1.0))
                    link(v.tensor_copy(idxf[0:NE, 0:CAP], idxu[0:NE, 0:CAP]))
                    v.tensor_scalar(idxf[0:NE, 0:CAP_LAT], idxf[0:NE, 0:CAP_LAT], float(NCTX), None, ALU.add).then_inc(s_gi, 1)
                    own(s_gi)
                    filled(dve, ("gi",))
                    v.tensor_copy(gT[0:CAP, :], pair(3)[0:CAP, 0:NE]).then_inc(s_gt, 1)
                    own(s_gt)
                    v.tensor_copy(iT[0:CAP, :], pair(3)[0:CAP, NE:2 * NE]).then_inc(s_gt, 1)
                    own(s_gt)
                    for dst, src in ((A2f, A2), (B2f, modc[:, 24:32, :])):
                        link(v.tensor_copy(dst[:, :, 0:CAP_LAT], src[:, :, 1:2].broadcast_to([P, KD, CAP_LAT])))
                        link(v.tensor_copy(dst[:, :, CAP_LAT:CAP], src[:, :, 0:1].broadcast_to([P, KD, CAP_CTX])))

            def elo(sl, ready, slot):
                dve.wait_ge(s_eh, ready)
                v.tensor_tensor(Wl[sl], eraw[slot], Wh[sl].bitcast(F32), ALU.subtract).then_inc(s_el, 1)

            def xmod(e):
                dve.wait_ge(s_xgT, e + 1)
                v.tensor_tensor(xgt3, xpsum, A2f, ALU.mult).then_inc(s_xgm, 1)
                dve.wait_ge(s_xgm, e + 1)
                v.tensor_tensor(xgt3, xgt3, B2f, ALU.add).then_inc(s_xgf, 1)
                dve.wait_ge(s_xgf, e + 1)

            def xlo(e):
                dve.wait_ge(s_xgh, e + 1)
                v.tensor_tensor(xl, xgt3, xh.bitcast(F32), ALU.subtract).then_inc(s_xgl, 1)

            def hidden(e, up_made):
                dve.wait_ge(s_silu, e + 1)
                dve.wait_ge(s_eu, up_made)
                v.tensor_tensor(aa[0:CAP, :], aa[0:CAP, :], pair(1)[0:CAP, :], ALU.mult).then_inc(s_a, 1)

            def alo(e):
                dve.wait_ge(s_ahi, e + 1)
                v.tensor_tensor(al, xpsum, ah.bitcast(F32), ALU.subtract).then_inc(s_alo, 1)

            def yout(e, first=False):
                dve.wait_ge(s_eu, min(e * 12 + 20, 12 * NE) if isinstance(e, int) else e * 12 + 20)
                if not first:
                    dve.wait_ge(s_scat, 16 * e)
                v.scalar_tensor_tensor(out=ye[0:CAP, :], in0=pair(2)[0:CAP, :], scalar=gT[0:CAP, bass.ds(e, 1)], in1=G2[0:CAP, :],
                                       op0=ALU.mult, op1=ALU.mult).then_inc(s_y, 1)

            def body(e, first=False, second=False, last=False):
                for j in range(12):
                    elo((j + 2) % NHL, e * 12 + (j - 3), (j + 2) % NRE)
                    if j == 3:
                        alo(e - 1)
                    if j == 4 and not first:
                        yout(e - 2, first=second)
                    if j == 9 and not last:
                        xmod(e + 1)
                    if j == 10:
                        if not last:
                            xlo(e + 1)
                        hidden(e, e * 12 + 4)

            dve.wait_ge(s_gt, 1)
            xmod(0)
            xlo(0)
            for n in range(8):
                elo(n % NHL, n + 1, n % NRE)
            xmod(1)
            xlo(1)
            hidden(0, 8)
            body(1, first=True)
            body(2, second=True)
            with dve.Fori(3, NE - 1) as e:
                body(e)
            body(NE - 1, last=True)
            elo(188 % NHL, 189, 188 % NRE)
            alo(NE - 1)
            elo(189 % NHL, 190, 189 % NRE)
            yout(NE - 2)
            elo(190 % NHL, 191, 190 % NRE)
            elo(191 % NHL, 192, 191 % NRE)
            yout(NE - 1)

        @block.tensor
        def _(pe):
            t = nc.tensor

            def mm3(out, s, m, start, stop):
                (sh, sl), (mh, ml) = s, m
                t.matmul(out, sh, mh, start=start, stop=False)
                t.matmul(out, sh, ml, start=False, stop=False)
                return t.matmul(out, sl, mh, start=False, stop=stop)

            def both(key, k):
                a, b = hl(key)
                return [w[:, 0:width(key)].rearrange("p (k n) -> p k n", k=k) for w in (a, b)]

            def rows_group(kind, g, s):
                key = (kind, g, s)
                pe.wait_ge(s_lo, SPLITNO[key] + 1)
                wh, wl = both(key, 4)
                for i in range(NT):
                    if s == 0:
                        begin(pe, (kind, g, i))
                    for kk in range(4):
                        kt = 4 * s + kk
                        if kind == "out" and g == 0 and i == 0:
                            pe.wait_ge(s_mgl, kt + 1)
                        tok = slice(P * i, P * i + P)
                        ins = mm3(bank(i), (act_hi[:, kt, tok], act_lo[:, kt, tok]), (wh[:, kk, :], wl[:, kk, :]), kt == 0, kt == 7)
                    if s == 1:
                        wrote(ins, (kind, g, i))
                if s == 0:
                    ins.then_inc(s_wused, 1)

            def columns(pr, wh, wl, a0, nk):
                for b in range(2):
                    ins = column_half(pr, b, wh, wl, a0, nk)
                return ins

            def column_half(pr, b, wh, wl, a0, nk):
                tok = slice(320 * b, 320 * b + 320)
                for kk in range(nk):
                    ins = mm3(bank(2 * pr + b)[:, 0:320], (wh[:, kk, :], wl[:, kk, :]),
                              (act_hi[:, a0 + kk, tok], act_lo[:, a0 + kk, tok]), kk == 0, kk == nk - 1)
                return ins

            def scores(n):
                h, i = ITER[n]
                for m in range(2):
                    r = slice(64 * m, 64 * m + 64)
                    begin(pe, ("s", n, m))
                    q = qT[r, h, P * i:P * i + P]
                    if i == 0:
                        ins = t.matmul(pair(m)[:, 0:P], q, kT[r, h, 0:P], start=True, stop=True)
                    else:
                        t.matmul(pair(m)[:, 0:512], q, kT[r, h, P:T], start=True, stop=True)
                        ins = t.matmul(pair(m)[:, 512:640], q, ckT[r, h, :], start=True, stop=True)
                    wrote(ins, ("s", n, m))

            pe.wait_ge(s_small, 32)
            for n, st in enumerate(STEPS):
                k = st[0]
                if k == "mod":
                    j = st[1]
                    if j == 0:
                        pe.wait_ge(s_cond, 1)
                    begin(pe, ("modrow", j))
                    for s in range(2):
                        landed(pe, ("mod", j, s))
                        w = rawv(("mod", j, s)).rearrange("p (k n) -> p k n", k=4)
                        for kk in range(4):
                            kt = 4 * s + kk
                            ins = t.matmul(bank(2 * modpair(j))[0:2, :], cond[:, kt, :], w[:, kk, :], start=kt == 0, stop=kt == 7)
                        if s == 0:
                            ins.then_inc(s_rused, 1)
                    wrote(ins, ("modrow", j))
                    if j not in LATE:
                        begin(pe, ("modcol", j))
                        for q in range(4):
                            ins = t.transpose(bank(2 * modpair(j) + 1)[:, 2 * q:2 * q + 2], mrow[0:2, P * q:P * q + P], ident[0:2, 0:2])
                        wrote(ins, ("modcol", j))
                    else:
                        if j == 11:
                            pe.wait_ge(s_brow11, 16)
                        else:
                            pe.wait_ge(s_brow, 16 * (LATE.index(j) + 1))
                        for w_ in ((0, 1) if j < 6 else (2,)):
                            key = ("g1", j, w_) if j < 6 else ("g2", j)
                            begin(pe, key)
                            t.matmul(bank(4), sel[0:2, w_, :], mrow[0:2, :], start=True, stop=False)
                            bias = brow11 if j == 11 else brow
                            wrote(t.matmul(bank(4), sel[0:1, 0, :], bias[0:1, :], start=False, stop=True), key)
                elif k == "xT":
                    i = st[1]
                    pe.wait_ge(s_xn, i + 1)
                    begin(pe, ("xT", i))
                    for q in range(KD):
                        ins = t.transpose(pair(3)[:, P * q:P * q + P], xt[i % 2][:, P * q:P * q + P], ident)
                    wrote(ins, ("xT", i))
                elif k == "split":
                    pe.wait_ge(s_hl, NT)
                elif k in ("tok", "out"):
                    rows_group(*st)
                elif k == "qkT":
                    g = st[1]
                    for i in range(NT):
                        pe.wait_ge(s_qr, 5 * g + i + 1)
                        begin(pe, ("qkT", g, i))
                        for h in range(H):
                            ins = t.transpose(pair(3)[:, P * h:P * h + P], yq[g][:, i, P * h:P * h + P], ident)
                        wrote(ins, ("qkT", g, i))
                elif k == "da":
                    n_ = st[1]
                    if n_ == -1:
                        pe.wait_ge(free[3], USE[("qkT", 1, NT - 1)][2])
                        pe.wait_ge(s_late, 48)
                    if n_ + 1 < NI:
                        scores(n_ + 1)
                    if 0 <= n_ - 1 < NI:
                        h, i = ITER[n_ - 1]
                        nt = NT if i else 1
                        if n_ >= 2:
                            pe.wait_ge(s_onb, n_ - 1)
                        pe.wait_ge(free[2], USE[("AT", n_ - 1)][2])
                        for j in range(nt):
                            hs = slice(P * h, P * h + P)
                            vals_ = vd[:, 0, hs] if i == 0 else (vd[:, 1 + j, hs] if j < 4 else cv[:, hs])
                            ins = t.matmul(bank(6)[:, 0:P], ATs[:, P * j:P * j + P], vals_, start=j == 0, stop=j == nt - 1)
                        ins.then_inc(s_pv, 1)
                    if 0 <= n_ < NI:
                        nt = NT if ITER[n_][1] else 1
                        pe.wait_ge(s_A, n_ + 1)
                        begin(pe, ("AT", n_))
                        for j in range(nt):
                            ins = t.transpose(pair(2)[:, P * j:P * j + P], pm[n_ % 2][0][:, P * j:P * j + P], ident)
                        wrote(ins, ("AT", n_))
                    if n_ >= 2:
                        pe.wait_ge(s_onb, n_ - 1)
                        if n_ > 2:
                            pe.wait_ge(s_oa, n_ - 2)
                        t.transpose(bank(7)[:, 0:P], onb, ident).then_inc(s_oaT, 1)
                elif k == "pf":
                    _, h, d, b = st
                    pe.wait_ge(s_lo, SPLITNO[("f", h)] + 1)
                    wh, wl = (w[:, 1024 * d:1024 * d + 1024].rearrange("p (k n) -> p k n", k=8) for w in hl(("f", h)))
                    if b == 0:
                        begin(pe, ("f", h, d))
                    ins = column_half(d, b, wh, wl, 0, 8)
                    if b == 1:
                        wrote(ins, ("f", h, d))
                elif k == "pq":
                    _, h, b = st
                    pe.wait_ge(s_lo, SPLITNO[("q", h)] + 1)
                    wh, wl = both(("q", h), 8)
                    if b == 0:
                        begin(pe, ("q", h))
                    ins = column_half(0, b, wh, wl, 0, 8)
                    if b == 1:
                        wrote(ins, ("q", h))
                elif k == "diag":
                    h = st[1]
                    pe.wait_ge(s_ksum, h + 1)
                    begin(pe, st)
                    for c in range(NT):
                        tok = slice(P * c, P * c + P)
                        ins = t.matmul(pair(1)[:, tok], Fb[:, 0, tok], qh[:, tok], start=True, stop=True)
                    wrote(ins, st)
                elif k == "lev":
                    h, lv = st[1], st[2]
                    pe.wait_ge(s_qk, LEVELS * h + lv + 1)
                    for d in range(2):
                        begin(pe, (*st, d))
                        for c in range(NT):
                            ins = t.matmul(bank(4 + 2 * (lv % 2) + d)[:, 64 * c:64 * c + 64], KS[lv % 2][:, d, P * c:P * c + P],
                                           QC[lv % 2][:, d, 64 * c:64 * c + 64],
                                           start=True, stop=True)
                        wrote(ins, (*st, d))
                elif k == "states":
                    h = st[1]
                    pe.wait_ge(s_ksb, h + 1)
                    for d in range(2):
                        begin(pe, ("kT", h, d))
                        for c in range(NT):
                            ins = t.transpose(pair(3)[:, P * c:P * c + P], KS[0][:, d, P * c:P * c + P], ident)
                        wrote(ins, ("kT", h, d))
                    hs = slice(P * h, P * h + P)
                    for d in range(2):
                        begin(pe, ("U", h, d))
                        pe.wait_ge(free[3], USE[("kT", h, d)][2])
                        for s, c in enumerate((0, 1, 2, 3) if d == 0 else (0, 4, 3, 2)):
                            ins = t.matmul(bank(4 + d)[:, P * s:P * s + P], Fb[:, d, P * c:P * c + P], v_hg[:, c, hs], start=True, stop=True)
                        wrote(ins, ("U", h, d))
                elif k == "o":
                    h = st[1]
                    hs = slice(P * h, P * h + P)
                    begin(pe, ("o", h))
                    pe.wait_ge(s_qb, h + 1)
                    pe.wait_ge(free[2], USE[("U", h, 1)][2])
                    for c in range(NT):
                        tok = slice(P * c, P * c + P)
                        ins = t.matmul(pair(3)[:, tok], attn[:, tok], v_hg[:, c, hs], start=True, stop=c == 0)
                        if c:
                            for d in range(2):
                                j = c - 1 if d == 0 else 4 - c
                                S = state0[:, d, h, :] if j == 0 else SC[:, d, j - 1, :]
                                ins = t.matmul(pair(3)[:, tok], QB[:, d, tok], S, start=False, stop=d == 1)
                    wrote(ins, ("o", h))
                elif k == "oT":
                    h = st[1]
                    pe.wait_ge(s_og, h + 1)
                    begin(pe, ("oT", h))
                    for c in range(NT):
                        ins = t.transpose(pair(3)[:, P * c:P * c + P], og[:, P * c:P * c + P], ident)
                    wrote(ins, ("oT", h))
                elif k == "gl":
                    c = st[1]
                    key = ("gl", c // 2)
                    pe.wait_ge(s_lo, SPLITNO[key] + 1)
                    wh, wl = (w[:, :, P * (c % 2):P * (c % 2) + P] for w in both(key, 8))
                    begin(pe, st)
                    wrote(columns(c % 2, wh, wl, 0, 8), st)
                elif k == "mrg":
                    c = st[1]
                    for b in range(2):
                        if c == 0:
                            pe.wait_ge(s_otl, 4 * b + 4)
                        key = ("br", b, c // 4)
                        pe.wait_ge(s_lo, SPLITNO[key] + 1)
                        wh, wl = (w[:, :, P * (c % 4):P * (c % 4) + P] for w in both(key, 4))
                        u = ("mx" if b == 0 else "my", c)
                        begin(pe, u)
                        wrote(columns(USE[u][0], wh, wl, 4 * b, 4), u)
                elif k == "h2T":
                    i = st[1]
                    if i < NT:
                        pe.wait_ge(s_xn2, i + 1)
                        begin(pe, ("h2T", i))
                        for q in range(KD):
                            ins = t.transpose(pair(USE[("h2T", i)][0])[:, P * q:P * q + P], xn2[i % 2][:, P * q:P * q + P], ident)
                        wrote(ins, ("h2T", i))
                    if i:
                        if i == 1:
                            begin(pe, ("rt",))
                        pe.wait_ge(s_h2, i)
                        for kt in range(KD):
                            ins = t.matmul(bank(0)[:, NE * (i - 1):NE * i], h2[(i - 1) % 2][:, kt, :], router[:, kt, :],
                                           start=kt == 0, stop=kt == KD - 1)
                        if i < NT:
                            ins.then_inc(s_rt, 1)
                        else:
                            wrote(ins, ("rt",))
                            pe.wait_ge(s_aff, 1)
                            begin(pe, ("affT",))
                            for j in range(NT):
                                ins = t.transpose(pair(1)[0:NE, P * j:P * j + P], aff[:, j, :], ident)
                            wrote(ins, ("affT",))
                elif k == "top":
                    pe.wait_ge(s_gi, 1)
                    begin(pe, ("gi",))
                    t.transpose(pair(3)[0:CAP, 0:NE], vals[0:NE, 0:CAP], ident[0:NE, 0:NE])
                    wrote(t.transpose(pair(3)[0:CAP, NE:2 * NE], idxf[0:NE, 0:CAP], ident[0:NE, 0:NE]), ("gi",))

            def turn_x(e, first=False):
                pe.wait_ge(s_gath, (e + 1) * 16)
                for q in range(KD):
                    ins = t.transpose(pair(3)[:, P * q:P * q + CAP], xg[0:CAP, P * q:P * q + P], ident[0:CAP, 0:CAP])
                ins.then_inc(s_xgT, 1)

            def piece_mm(pr, ready, sl, hi_, lo_, j):
                pe.wait_ge(s_el, ready)
                wh, wl = (w[sl].rearrange("p (k n) -> p k n", k=2) for w in (Wh, Wl))
                for kk in range(2):
                    kt = 2 * j + kk
                    for b in range(2):
                        cs = slice(512 * b, 512 * b + 512)
                        ins = mm3(bank(2 * pr + b)[0:CAP, :], (hi_[:, kt, :], lo_[:, kt, :]), (wh[:, kk, cs], wl[:, kk, cs]), kt == 0, kt == 7)
                ins.then_inc(s_eu, 1)

            def turn_a(e):
                pe.wait_ge(s_a, e + 1)
                for q in range(KD):
                    ins = t.transpose(pair(3)[:, P * q:P * q + CAP], aa[0:CAP, P * q:P * q + P], ident[0:CAP, 0:CAP])
                ins.then_inc(s_aT, 1)

            def body(e, first=False, last=False):
                for j in range(12):
                    m, q = j // 4, j % 4
                    if j == 0:
                        pe.wait_ge(s_silu, e)
                    if j == 4:
                        pe.wait_ge(s_a, e)
                    if j == 6 and not last:
                        pe.wait_ge(s_alo, e)
                        turn_x(e + 1)
                    if j == 8:
                        pe.wait_ge(s_alo, e)
                        if not first:
                            pe.wait_ge(s_y, e - 1)
                    hi_, lo_ = (xh, xl) if m < 2 else (ah, al)
                    if j == 0:
                        pe.wait_ge(s_xgl, e + 1)
                    piece_mm(m, e * 12 + (j - 3), (j + 2) % NHL, hi_, lo_, q)
                if not last:
                    pe.wait_ge(s_xgm, e + 2)
                turn_a(e)

            turn_x(0)
            pe.wait_ge(s_xgl, 1)
            for n in range(8):
                piece_mm(n // 4, n + 1, n % NHL, xh, xl, n % 4)
            pe.wait_ge(s_xgm, 1)
            turn_x(1)
            pe.wait_ge(s_xgm, 2)
            turn_a(0)
            body(1, first=True)
            with pe.Fori(2, NE - 1) as e:
                body(e)
            body(NE - 1, last=True)
            pe.wait_ge(s_alo, NE)
            pe.wait_ge(s_y, NE - 1)
            for q in range(4):
                piece_mm(2, 189 + q, (188 + q) % NHL, ah, al, q)


_INS = ['x_prompt', 'x_sample', 'cache_v', 'state_hgrn', 'w_mod', 'b_mod', 'w_in', 'diff_lambda', 'w_branch_hgrn', 'w_branch_attn', 'w_out', 'router_w', 'w_exp_gate', 'w_exp_up', 'w_exp_down']
_OUTS = [((1, 128, 1024), 'float32'), ((1, 512, 1024), 'float32'), ((1, 1, 128, 4, 2, 64), 'float32'),
         ((1, 1, 128, 4, 128), 'float32'), ((1, 1, 2, 4, 128, 128), 'float32')]


def tables():
    import numpy as np
    c = np.zeros((P, K_N), np.float32)
    c[:, K_ID:K_ID + P] = np.eye(P)
    s = np.arange(P)
    m = np.zeros((P, 2, LEVELS, 64), np.float32)
    for lv in range(LEVELS):
        half = 64 >> lv
        for j in range(64):
            same = s // (2 * half) == j // half
            second = (s % (2 * half)) >= half
            m[:, 0, lv, j] = same & ~second
            m[:, 1, lv, j] = same & second
    c[:, K_MASK:K_MASK + 14 * 64] = m.reshape(P, -1)
    c[:, K_RESET:K_RESET + T] = (np.arange(T) % P != 0)
    f = np.float32(10000.0) ** (-np.arange(16, dtype=np.float32) / np.float32(16))
    tok = np.arange(NLAT)
    ang = np.stack([(tok // 64).astype(np.float32)[:, None] * f, (tok % 64).astype(np.float32)[:, None] * f], 1)
    co, si = np.cos(ang), np.sin(ang)
    co = np.stack([co, co], 2).reshape(4, P, 64)
    si = np.stack([-si, si], 2).reshape(4, P, 64)
    c[:, K_COS:K_COS + 256] = co.transpose(1, 0, 2).reshape(P, 256)
    c[:, K_SIN:K_SIN + 256] = si.transpose(1, 0, 2).reshape(P, 256)
    c[0, K_SEL:K_SEL + 128] = 1
    c[1, K_SEL + 128:K_SEL + 256] = 1
    c[1, K_SEL + 256:K_SEL + 256 + CAP_LAT] = 1
    c[0, K_SEL + 256 + CAP_LAT:K_SEL + 256 + CAP] = 1
    return c


def columns_of(x):
    import numpy as np

    def by_p(a, k):
        return np.moveaxis(a.reshape(-1, k, P), 2, 0)

    parts = [by_p(x["norm1_w"], 8), by_p(x["norm2_w"], 8),
             np.stack([by_p(x["c_ctx"], 8)[:, 0], by_p(x["c"], 8)[:, 0]], 2),
             by_p(x["b_mod"], 48), by_p(x["b_gate"], 16), x["hgrn_norm_w"][0].T, x["diff_subln_w"].T,
             by_p(x["hgrn_lb_logits"], 4), np.broadcast_to(x["qk_norm_w"].reshape(1, 128), (P, 128))]
    return np.ascontiguousarray(np.concatenate([a.reshape(P, -1) for a in parts], 1))


def kernel(**inputs):
    import numpy as _np
    import concourse.bacc as _bacc
    from concourse import mybir as _mybir
    from concourse.bass_utils import run_bass_kernel_spmd as _run

    nc = _bacc.Bacc("TRN2", target_bir_lowering=False, num_devices=1)
    arrays, A = {}, {}
    for name in _INS:
        a = _np.ascontiguousarray(inputs[name])
        arrays[f"in_{name}_dram"] = a
        A[name] = nc.dram_tensor(f"in_{name}_dram", a.shape, _mybir.dt.from_np(a.dtype), kind="ExternalInput").ap()
    x = {n: _np.asarray(a) for n, a in inputs.items()}
    laid = {"const": tables(), "cols": columns_of(x),
            "ckT": _np.ascontiguousarray(x["cache_k"].reshape(NPAST, H, 2 * DQK).transpose(2, 1, 0).reshape(P, H * NPAST))}
    for name, a in laid.items():
        arrays[name + "_dram"] = a
        A[name] = nc.dram_tensor(name + "_dram", a.shape, F32, kind="ExternalInput").ap()
    outs = []
    for i, (shape, dtype) in enumerate(_OUTS):
        dt = _mybir.dt.from_np(_np.dtype(dtype))
        outs.append(nc.dram_tensor(f"out_{i}_dram", shape, dt, kind="ExternalOutput").ap())
    fused_step(nc, A, outs)
    r = _run(nc, [arrays], core_ids=[0])
    return tuple(r.results[0][f"out_{i}_dram"] for i in range(len(_OUTS)))
```
